# Optimizing a Trainium2 kernel written in Bass

```python
import math
import jax, jax.numpy as jnp
from jax import lax
import numpy as np

D_MODEL = 1024
BATCH = 1
SEQ = 2048
DEPTH = 2
DEC_BATCH = 1
DEC_SEQ = 32
PAST_LEN = 2048

CHUNK = 64
Q_BLOCK = 128
HEAD_DIM = 64
D_MIX = D_MODEL
A_WIDTH = D_MIX // 2
A_HEADS = A_WIDTH // HEAD_DIM
A_KV_HEADS = A_HEADS // 4
A_GROUP = A_HEADS // A_KV_HEADS
IDX_HEADS = A_HEADS
IDX_DIM = HEAD_DIM
IDX_W_SCALE = (IDX_HEADS * IDX_DIM) ** -0.5
TOPK_MAX = 256
B_WIDTH = D_MIX // 4
B_HEADS = B_WIDTH // HEAD_DIM
C_WIDTH = D_MIX // 4
C_HEADS = C_WIDTH // HEAD_DIM
ROPE_THETA = 10000.0
EPS = 1e-6

_SIZES = (A_WIDTH, A_KV_HEADS * HEAD_DIM, A_KV_HEADS * HEAD_DIM, A_WIDTH,
          IDX_HEADS * IDX_DIM, IDX_DIM, IDX_HEADS,
          B_WIDTH, B_WIDTH, B_WIDTH, B_WIDTH,
          C_WIDTH, C_WIDTH, C_WIDTH, C_WIDTH)
SPLIT_IDX = tuple(int(s) for s in np.cumsum(_SIZES)[:-1])
N_IN = int(sum(_SIZES))

kernel_name = 'hymba_dsa_hgrn2_retention_stream_step'

def rms_norm(x, g):
    xf = x.astype(jnp.float32)
    y = xf * lax.rsqrt(jnp.mean(xf * xf, axis=-1, keepdims=True) + EPS) * g.astype(jnp.float32)
    return y.astype(x.dtype)

def rope(x, pos):
    half = x.shape[-1] // 2
    freqs = ROPE_THETA ** (-jnp.arange(half, dtype=jnp.float32) / half)
    ang = pos.astype(jnp.float32)[:, None] * freqs[None, :]
    cos = jnp.cos(ang)[None, :, None, :]
    sin = jnp.sin(ang)[None, :, None, :]
    xf = x.astype(jnp.float32)
    x1, x2 = xf[..., :half], xf[..., half:]
    return jnp.concatenate([x1 * cos - x2 * sin, x2 * cos + x1 * sin], axis=-1).astype(x.dtype)

def dsa_block(q, qi, w, qpos, k_all, v_all, ki_all, topk):
    f32 = jnp.float32
    kpos = jnp.arange(k_all.shape[1])
    sc = jnp.einsum('bthd,bsd->bths', qi.astype(f32), ki_all.astype(f32))
    sc = jnp.einsum('bths,bth->bts', jax.nn.relu(sc), w.astype(f32))
    admissible = (kpos[None, :] // CHUNK) <= (qpos[:, None] // CHUNK)
    sc = jnp.where(admissible[None], sc, -jnp.inf)
    vals, idx = lax.top_k(sc, topk)
    valid = jnp.isfinite(vals)
    gather = jax.vmap(lambda rows, ii: rows[ii])
    kg = gather(k_all, idx)
    vg = gather(v_all, idx)
    b, t = q.shape[:2]
    qg = q.reshape(b, t, A_KV_HEADS, A_GROUP, HEAD_DIM)
    logits = jnp.einsum('bthgd,btshd->bthgs', qg, kg).astype(f32) * (HEAD_DIM ** -0.5)
    logits = jnp.where(valid[:, :, None, None, :], logits, -jnp.inf)
    p = jax.nn.softmax(logits, axis=-1).astype(vg.dtype)
    o = jnp.einsum('bthgs,btshd->bthgd', p, vg)
    return o.reshape(b, t, A_WIDTH)

def sparse_attention(q, qi, w, qpos, k_all, v_all, ki_all):
    b, t = q.shape[:2]
    topk = min(TOPK_MAX, k_all.shape[1] // 4)
    if t > Q_BLOCK and t % Q_BLOCK == 0:
        nb = t // Q_BLOCK
        blk = lambda a: a.reshape((b, nb, Q_BLOCK) + a.shape[2:]).swapaxes(0, 1)
        out = lax.map(lambda xs: dsa_block(xs[0], xs[1], xs[2], xs[3], k_all, v_all, ki_all, topk),
                      (blk(q), blk(qi), blk(w), qpos.reshape(nb, Q_BLOCK)))
        return out.swapaxes(0, 1).reshape(b, t, A_WIDTH)
    return dsa_block(q, qi, w, qpos, k_all, v_all, ki_all, topk)

def gla_chunk(S, xs):
    q, k, v, logf = xs
    c = q.shape[1]
    bcum = jnp.cumsum(logf, axis=1)
    causal = jnp.tril(jnp.ones((c, c), dtype=bool))
    diff = bcum[:, :, None] - bcum[:, None]
    dec = jnp.exp(jnp.where(causal[None, :, :, None, None], diff, -jnp.inf))
    att = jnp.einsum('bthk,bshk,btshk->bths', q, k, dec)
    o = jnp.einsum('bths,bshv->bthv', att, v) + jnp.einsum('bthk,bhkv->bthv', q * jnp.exp(bcum), S)
    b_last = bcum[:, -1]
    S_new = jnp.exp(b_last)[..., None] * S + jnp.einsum('bshk,bshv->bhkv', k * jnp.exp(b_last[:, None] - bcum), v)
    return S_new, o

def retention_log_decay():
    return jnp.log(1.0 - jnp.exp(jnp.linspace(math.log(1.0 / 32), math.log(1.0 / 512), C_HEADS, dtype=jnp.float32)))

def ret_chunk(R, xs):
    q, k, v = xs
    lg = retention_log_decay()
    c = q.shape[1]
    n = jnp.arange(c, dtype=jnp.float32)
    diff = n[:, None] - n[None, :]
    causal = diff >= 0
    dmat = jnp.where(causal[None], jnp.exp(jnp.where(causal, diff, 0.0)[None] * lg[:, None, None]), 0.0)
    att = jnp.einsum('bthk,bshk->bhts', q, k) * dmat[None]
    inner_scale = jnp.exp((n[:, None] + 1.0) * lg[None, :])
    o = jnp.einsum('bhts,bshv->bthv', att, v) + jnp.einsum('bthk,bhkv->bthv', q, R) * inner_scale[None, :, :, None]
    k_scale = jnp.exp((c - 1.0 - n)[:, None] * lg[None, :])
    R_new = jnp.exp(c * lg)[None, :, None, None] * R + jnp.einsum('bshk,bshv->bhkv', k * k_scale[None, :, :, None], v)
    return R_new, o

def chunked_scan(step, S0, xs):
    t = xs[0].shape[1]
    if t <= CHUNK:
        return step(S0, xs)
    nc = t // CHUNK
    xs_c = tuple(a.reshape((a.shape[0], nc, CHUNK) + a.shape[2:]).swapaxes(0, 1) for a in xs)
    S, o = lax.scan(step, S0, xs_c)
    o = o.swapaxes(0, 1)
    return S, o.reshape((o.shape[0], t) + o.shape[3:])

def mixer_layer(x, pos, k_past, v_past, ik_past, s_hgrn, s_ret, lb,
                norm_g, w_in, q_norm_g, k_norm_g, hgrn_norm_g, ret_norm_g, w_out):
    f32 = jnp.float32
    b, t, _ = x.shape
    h = rms_norm(x, norm_g)
    proj = jnp.einsum('btd,dn->btn', h, w_in)
    (aq, ak, av, ag, iq, ik, iw, bq, bf, bi, bg, cq, ck, cv, cg) = jnp.split(proj, SPLIT_IDX, axis=-1)

    aq = rope(rms_norm(aq.reshape(b, t, A_HEADS, HEAD_DIM), q_norm_g), pos)
    ak = rope(rms_norm(ak.reshape(b, t, A_KV_HEADS, HEAD_DIM), k_norm_g), pos)
    av = av.reshape(b, t, A_KV_HEADS, HEAD_DIM)
    iq = rope(iq.reshape(b, t, IDX_HEADS, IDX_DIM), pos)
    ik = rope(ik.reshape(b, t, 1, IDX_DIM), pos)[:, :, 0]
    k_all = jnp.concatenate([k_past.astype(ak.dtype), ak], axis=1)
    v_all = jnp.concatenate([v_past.astype(av.dtype), av], axis=1)
    ik_all = jnp.concatenate([ik_past.astype(ik.dtype), ik], axis=1)
    ya = sparse_attention(aq, iq, iw * IDX_W_SCALE, pos, k_all, v_all, ik_all) * jax.nn.silu(ag)

    f = lb + (1.0 - lb) * jax.nn.sigmoid(bf.astype(f32))
    heads_b = lambda a: a.reshape(b, t, B_HEADS, HEAD_DIM)
    s_hgrn_new, ob = chunked_scan(gla_chunk, s_hgrn.astype(f32),
                                  (heads_b(bq.astype(f32)), heads_b(1.0 - f), heads_b(bi.astype(f32)), heads_b(jnp.log(f))))
    yb = rms_norm(ob, hgrn_norm_g).reshape(b, t, B_WIDTH).astype(x.dtype) * jax.nn.silu(bg)

    cq = rope(cq.reshape(b, t, C_HEADS, HEAD_DIM), pos).astype(f32)
    ck = rope(ck.reshape(b, t, C_HEADS, HEAD_DIM), pos).astype(f32) * (HEAD_DIM ** -0.5)
    cv = cv.reshape(b, t, C_HEADS, HEAD_DIM).astype(f32)
    s_ret_new, oc = chunked_scan(ret_chunk, s_ret.astype(f32), (cq, ck, cv))
    yc = rms_norm(oc, ret_norm_g).reshape(b, t, C_WIDTH).astype(x.dtype) * jax.nn.silu(cg)

    y = jnp.concatenate([ya, yb.astype(ya.dtype), yc.astype(ya.dtype)], axis=-1)
    out = x + jnp.einsum('btm,md->btd', y, w_out)
    return out, (ak, av, ik, s_hgrn_new, s_ret_new)

def setup_inputs(seed: int = 0) -> dict:
    key = jax.random.key(seed)
    ks = jax.random.split(key, 16)
    nrm = jax.random.normal
    f32 = jnp.float32
    return {
        'x_prompt': nrm(ks[0], (BATCH, SEQ, D_MODEL), f32),
        'x_sample': nrm(ks[1], (DEC_BATCH, DEC_SEQ, D_MODEL), f32),
        'cache_k': nrm(ks[2], (DEPTH, DEC_BATCH, PAST_LEN, A_KV_HEADS, HEAD_DIM), f32),
        'cache_v': nrm(ks[3], (DEPTH, DEC_BATCH, PAST_LEN, A_KV_HEADS, HEAD_DIM), f32),
        'cache_idx_k': nrm(ks[4], (DEPTH, DEC_BATCH, PAST_LEN, IDX_DIM), f32),
        'state_hgrn': 0.5 * nrm(ks[5], (DEPTH, DEC_BATCH, B_HEADS, HEAD_DIM, HEAD_DIM), f32),
        'state_ret': 4.0 * nrm(ks[6], (DEPTH, DEC_BATCH, C_HEADS, HEAD_DIM, HEAD_DIM), f32),
        'norm_g': 1.0 + 0.02 * nrm(ks[7], (DEPTH, D_MODEL), f32),
        'w_in': nrm(ks[8], (DEPTH, D_MODEL, N_IN), f32) * (D_MODEL ** -0.5),
        'q_norm_g': 1.0 + 0.02 * nrm(ks[9], (DEPTH, HEAD_DIM), f32),
        'k_norm_g': 1.0 + 0.02 * nrm(ks[10], (DEPTH, HEAD_DIM), f32),
        'hgrn_lb_logits': 0.5 * nrm(ks[11], (DEPTH, B_WIDTH), f32),
        'hgrn_norm_g': 1.0 + 0.02 * nrm(ks[12], (DEPTH, HEAD_DIM), f32),
        'ret_norm_g': 1.0 + 0.02 * nrm(ks[13], (DEPTH, HEAD_DIM), f32),
        'w_out': nrm(ks[14], (DEPTH, D_MIX, D_MODEL), f32) * (D_MIX ** -0.5),
    }

def reference(x_prompt, x_sample, cache_k, cache_v, cache_idx_k, state_hgrn, state_ret,
              norm_g, w_in, q_norm_g, k_norm_g, hgrn_lb_logits, hgrn_norm_g, ret_norm_g, w_out):
    f32 = jnp.float32
    sm = jax.nn.softmax(hgrn_lb_logits.astype(f32), axis=0)
    lbs = jnp.cumsum(sm, axis=0) - sm[0:1]

    bp, tp = x_prompt.shape[0], x_prompt.shape[1]
    bs, ts = x_sample.shape[0], x_sample.shape[1]
    past = cache_k.shape[2]
    pos_p = jnp.arange(tp)
    pos_s = past + jnp.arange(ts)
    empty_k = jnp.zeros((bp, 0, A_KV_HEADS, HEAD_DIM), x_prompt.dtype)
    empty_ik = jnp.zeros((bp, 0, IDX_DIM), x_prompt.dtype)
    zero_hg = jnp.zeros((bp, B_HEADS, HEAD_DIM, HEAD_DIM), f32)
    zero_rt = jnp.zeros((bp, C_HEADS, HEAD_DIM, HEAD_DIM), f32)

    yp, ys = x_prompt, x_sample
    pk, pv, pik, phg, prt = [], [], [], [], []
    sk, sv, sik, shg, srt = [], [], [], [], []
    for l in range(DEPTH):
        w_l = (norm_g[l], w_in[l], q_norm_g[l], k_norm_g[l], hgrn_norm_g[l], ret_norm_g[l], w_out[l])
        yp, (k_, v_, ik_, hg_, rt_) = mixer_layer(yp, pos_p, empty_k, empty_k, empty_ik, zero_hg, zero_rt, lbs[l], *w_l)
        pk.append(k_); pv.append(v_); pik.append(ik_); phg.append(hg_); prt.append(rt_)
        ys, (k_, v_, ik_, hg_, rt_) = mixer_layer(ys, pos_s, cache_k[l], cache_v[l], cache_idx_k[l],
                                                   state_hgrn[l], state_ret[l], lbs[l], *w_l)
        sk.append(k_); sv.append(v_); sik.append(ik_); shg.append(hg_); srt.append(rt_)

    return (yp, ys,
            jnp.stack(pk), jnp.stack(pv), jnp.stack(pik), jnp.stack(phg), jnp.stack(prt),
            jnp.stack(sk), jnp.stack(sv), jnp.stack(sik), jnp.stack(shg), jnp.stack(srt))


_drawn_inputs = setup_inputs


def setup_inputs(seed=0):
    import zlib

    import numpy as np

    out = dict(_drawn_inputs(seed))
    spreads = {}
    factors = {'q_norm_g': 27.395, 'hgrn_norm_g': 7.044, 'ret_norm_g': 6.365}
    for name, (base, spread) in spreads.items():
        noise = np.random.default_rng([zlib.crc32(name.encode()), seed]).standard_normal(out[name].shape)
        drawn = base * np.exp(spread * noise) if base else spread * noise
        out[name] = __import__('jax').numpy.asarray(drawn.astype(out[name].dtype))
    for name, factor in factors.items():
        out[name] = (out[name] * factor).astype(out[name].dtype)
    return out
```

```python
from contextlib import ExitStack

import numpy as np
import concourse.bass as bass
from concourse import mybir

F32 = mybir.dt.float32
BF16 = mybir.dt.bfloat16
I32 = mybir.dt.int32
ALU = mybir.AluOpType
ACT = mybir.ActivationFunctionType
AX_X = mybir.AxisListType.X

P = 128
HD = 64
HALF = HD // 2
CHUNK = 64
A_HEADS, KV_HEADS = 8, 2
GRP = A_HEADS // KV_HEADS
EPS = 1e-6
IDX_W_SCALE = (A_HEADS * HD) ** -0.5
WIN = 32
NIT = 24
BIG = 1e30
MASKED = 30000.0

GROUPS = [("bqf", 512), ("big", 512), ("cqk", 512), ("cvg", 512), ("iq", 512), ("kvi", 328), ("aq", 512), ("ag", 512)]
GI = {n: i for i, (n, _) in enumerate(GROUPS)}
GOFF = {n: sum(w for _, w in GROUPS[:i]) for i, (n, _) in enumerate(GROUPS)}
N_IN = sum(w for _, w in GROUPS)
NG = len(GROUPS)
PJ_BANKS = 4
ACT_G = {"bqf": 1, "big": 2, "cvg": 3, "aq": 4, "ag": 5}
DVE_G = {"big": 1, "cqk": 2, "cvg": 3, "iq": 4, "kvi": 5, "aq": 6, "ag": 7}
DVE_STEPS = 55


class Steps:

    def __init__(self, eng, sem, base=0):
        self.eng, self.sem, self.base, self.n = eng, sem, base, 0

    def __call__(self, ins):
        self.n += 1
        ins.then_inc(self.sem, 1)
        self.eng.wait_ge(self.sem, self.base + self.n)


def build(nc, xin, cache_k, cache_v, cache_i, st_h, st_r, norm_g, w_in, q_g, k_g, lb_logits, h_g, r_g, w_out,
          c_rope, c_ident, c_causal, c_dmat, c_lrow, c_ksc, c_gt, c_bmask, c_pow,
          xs, k_p, v_p, ik_p, hg_p, rt_p, k_s, v_s, ik_s, hg_s, rt_s):
    DEPTH, D = w_in.shape[0], w_out.shape[3]
    DC = D // P
    SEQ = k_p.shape[1]
    TS = k_s.shape[1]
    PAST = cache_k.shape[2]
    NB = SEQ // P
    NPB = PAST // P
    K_P, K_S = min(256, SEQ // 4), min(256, (PAST + TS) // 4)
    NBLK = NB + 1

    def scratch(name, shape):
        return nc.dram_tensor(name, shape, F32, kind="Internal").ap()

    kT_d, ikT_d = scratch("kT_d", [P, SEQ + TS]), scratch("ikT_d", [P, SEQ + TS])
    qT_d, iqT_d = scratch("qT_d", [NBLK, P, 4 * P]), scratch("iqT_d", [NBLK, P, 4 * P])
    iw_d, y_d = scratch("iw_d", [NBLK, P, 8]), scratch("y_d", [NBLK, P, D])

    def rows(b):
        return (b * P, P) if b < NB else (SEQ, TS)

    def recurrent_half(l, sem):
        with ExitStack() as ctx:
            def sb(name, shape, dt=F32):
                return ctx.enter_context(nc.sbuf_tensor(name, shape, dt))

            w = sb("w_in_sb", [P, DC * N_IN])
            rope = sb("rope", [P, NBLK, HD])
            causal = sb("causal", [P, P])
            dmat = sb("dmat", [P, 4, P])
            lrow = sb("lrow", [P, 2, P])
            ksc = sb("ksc", [P, 2, 4])
            gt = sb("gt", [P, 2, 2])
            bmask = sb("bmask", [P, P])
            ng = sb("ng", [P, DC])
            qg, kg = sb("qg", [P, HD]), sb("kg", [P, HD])
            hg, rg = sb("hg", [P, HD]), sb("rg", [P, HD])
            x = sb("x", [P, D])
            hT = sb("hT", [P, DC, P])
            bqf = sb("bqf", [P, 4, P])
            bi, egb, gb = sb("bi", [P, 256]), sb("egb", [P, 256]), sb("gb", [P, 256])
            cv, egc, gc = sb("cv", [P, 256]), sb("egc", [P, 256]), sb("gc", [P, 256])
            bqT, ef, fT = sb("bqT", [P, 2, P]), sb("ef", [P, 2, P]), sb("fT", [P, 2, P])
            kkT, bT = sb("kkT", [P, 2, P]), sb("bT", [P, 2, P])
            qe, qw, bw = sb("qe", [P, 2, P]), sb("qw", [P, 2, P]), sb("bw", [P, 2, P])
            kt = sb("kt", [P, 2, 4, P])
            k2T, k2, elast = sb("k2T", [P, 2, P]), sb("k2", [P, 2, P]), sb("elast", [P, 2])
            ones = sb("ones", [P, P])
            rt1, rt2 = sb("rt1", [P, 512]), sb("rt2", [P, 512])
            rpc, cks = sb("rpc", [P, 512]), sb("cks", [P, 256])
            cqkT, cqs = sb("cqkT", [P, 4, P]), sb("cqs", [P, 2, P])
            atth, attr = sb("atth", [P, 4, P]), sb("attr", [P, 4, P])
            rpi = sb("rpi", [P, 512])
            av, iw, ik2 = sb("av", [P, P]), sb("iw", [P, 8]), sb("ik2", [P, P])
            ak, sqk, ssk, rsk = sb("ak", [P, P]), sb("sqk", [P, P]), sb("ssk", [P, 2]), sb("rsk", [P, 2])
            aq, ssa, rsa = sb("aq", [P, 512]), sb("ssa", [P, 8]), sb("rsa", [P, 8])
            ega, ga = sb("ega", [P, 512]), sb("ga", [P, 512])
            sqo = sb("sqo", [P, 256])
            sso, rso = sb("sso", [P, 2, 4]), sb("rso", [P, 2, 4])
            yb, yc, ut = sb("yb", [P, 256]), sb("yc", [P, 256]), sb("ut", [P, 256])
            S2, R2 = sb("S2", [P, 2, P]), sb("R2", [P, 2, P])
            iqT, qT, kiT = sb("iqT", [P, 4, P]), sb("qT", [P, 4, P]), sb("kiT", [P, 2, P])
            ssx, rsx = sb("ssx", [P, 1]), sb("rsx", [P, 1])
            mhalf = sb("mhalf", [P, 8])
            lbl = sb("lbl", [P, 2, 2])
            sqa, junk = sb("sqa", [P, 512]), sb("junk", [P, D], BF16)

            def ps(name):
                return ctx.enter_context(nc.psum_tensor(name, [P, 512], F32))

            PJ = [ps(f"PJ{i}") for i in range(PJ_BANKS)]
            TR = [ps("TR0"), ps("TR1")]
            ATT, OU = ps("ATT"), ps("OU")
            trv = [t[:].rearrange("p (c t) -> p c t", c=4) for t in TR]

            consts, states_in, x_in = sem("consts"), sem("states_in"), sem("x_in")
            w_in_s = [sem(f"w_{n}") for n, _ in GROUPS]
            prep = sem("prep")
            x_sq, x_ms, x_rs, h_ok, xT_ok, hT_ok = (sem(n) for n in ("x_sq", "x_ms", "x_rs", "h_ok", "xT_ok", "hT_ok"))
            proj, act_read, dve_read = sem("proj"), sem("act_read"), sem("dve_read")
            bqfT_ok, bq_copied, ef_ok, f_ok, lf_ok, b_ok, eb_ok, kt_ok, hq_ok = (sem(n) for n in (
                "bqfT_ok", "bq_copied", "ef_ok", "f_ok", "lf_ok", "b_ok", "eb_ok", "kt_ok", "hq_ok"))
            k2t_ok, k2_ok, atth_ok, atth_m = (sem(n) for n in ("k2t_ok", "k2_ok", "atth_ok", "atth_m"))
            rpc_ok, cqkT_ok, cqkT_c, cqs_ok, attr_ok, attr_m = (sem(n) for n in (
                "rpc_ok", "cqkT_ok", "cqkT_c", "cqs_ok", "attr_ok", "attr_m"))
            oh_ok, or_ok, sqo_ok, msoh, rsoh, sh_ok, yb_ok = (sem(n) for n in (
                "oh_ok", "or_ok", "sqo_ok", "msoh", "rsoh", "sh_ok", "yb_ok"))
            rpi_ok, iqT_ok, iqT_c = sem("rpi_ok"), sem("iqT_ok"), sem("iqT_c")
            sqk_ok, msk, rsk_ok, ki_ok, kiT_ok, kiT_c, av_ok = (sem(n) for n in (
                "sqk_ok", "msk", "rsk_ok", "ki_ok", "kiT_ok", "kiT_c", "av_ok"))
            sqa_ok, msa, rsa_ok, aq_ok, aqT_ok, aqT_c = (sem(n) for n in (
                "sqa_ok", "msa", "rsa_ok", "aq_ok", "aqT_ok", "aqT_c"))
            dve_step, even_heads = sem("dve_step"), sem("even_heads")
            st_q, st_iq, st_ki, st_k, st_v, st_y, st_st = (sem(n) for n in (
                "st_q", "st_iq", "st_ki", "st_k", "st_v", "st_y", "st_st"))

            def wait(eng, s, value):
                if isinstance(value, int) and value <= 0:
                    return
                eng.wait_ge(s, value)

            block = ctx.enter_context(nc.Block())

            @block.sync
            def _(sp):
                def load_x(b):
                    r0, T = rows(b)
                    sp.dma_start(x[0:T, :], xs[l, r0:r0 + T, :]).then_inc(x_in, 16)

                load_x(0)
                for d, s in ((rope[:], c_rope[:, :, :]), (causal[:], c_causal[:, :]), (dmat[:], c_dmat[:, :, :]),
                             (lrow[:], c_lrow[:, :, :]), (ksc[:], c_ksc[:, :, :]), (gt[:], c_gt[:, :, :]),
                             (bmask[:], c_bmask[:, :]), (ng[:], norm_g[l, :, :]),
                             (qg[:], q_g[l, :, :]), (kg[:], k_g[l, :, :]), (hg[:], h_g[l, :, :]), (rg[:], r_g[l, :, :])):
                    sp.dma_start(d, s).then_inc(consts, 16)
                for g, (n, wd) in enumerate(GROUPS):
                    cols = slice(DC * GOFF[n], DC * (GOFF[n] + wd))
                    sp.dma_start(w[:, cols], w_in[l, :, cols]).then_inc(w_in_s[g], 16)
                for b in range(NBLK):
                    r0, T = rows(b)
                    dst_k, dst_v, dst_i = (k_p, v_p, ik_p) if b < NB else (k_s, v_s, ik_s)
                    o0 = r0 if b < NB else 0
                    if b == NB:
                        sp.wait_ge(sh_ok, 2 * NB)
                        for j in range(4):
                            sp.dma_start(hg_p[l, j, :, :], S2[64 * (j % 2):64 * (j % 2) + 64, j // 2, 64 * (j % 2):64 * (j % 2) + 64]).then_inc(st_st, 16)
                            sp.dma_start(rt_p[l, j, :, :], R2[64 * (j % 2):64 * (j % 2) + 64, j // 2, 64 * (j % 2):64 * (j % 2) + 64]).then_inc(st_st, 16)
                        sp.wait_ge(st_st, 8 * 16)
                        for j in range(4):
                            sp.dma_start(S2[64 * (j % 2):64 * (j % 2) + 64, j // 2, 64 * (j % 2):64 * (j % 2) + 64], st_h[l, j, :, :]).then_inc(states_in, 16)
                            sp.dma_start(R2[64 * (j % 2):64 * (j % 2) + 64, j // 2, 64 * (j % 2):64 * (j % 2) + 64], st_r[l, j, :, :]).then_inc(states_in, 16)
                    if b < NB:
                        sp.wait_ge(xT_ok, 2 * b + 2)
                        load_x(b + 1)
                    sp.wait_ge(yb_ok, 2 * b + 1)
                    sp.dma_start(y_d[b, 0:T, 512:768], yb[0:T, :]).then_inc(st_y, 16)
                    sp.wait_ge(iqT_c, b + 1)
                    sp.dma_start(iqT_d[b, :, 0:4 * T], iqT[:, :, 0:T]).then_inc(st_iq, 16)
                    sp.wait_ge(av_ok, b + 1)
                    sp.dma_start(dst_v[l, o0:o0 + T, :], av[0:T, :]).then_inc(st_v, 16)
                    sp.dma_start(iw_d[b, 0:T, :], iw[0:T, :]).then_inc(st_v, 16)
                    sp.wait_ge(ki_ok, b + 1)
                    sp.dma_start(dst_k[l, o0:o0 + T, :], ak[0:T, :]).then_inc(st_k, 16)
                    sp.dma_start(dst_i[l, o0:o0 + T, :], ik2[0:T, 0:HD]).then_inc(st_k, 16)
                    sp.wait_ge(yb_ok, 2 * b + 2)
                    sp.dma_start(y_d[b, 0:T, 768:1024], yc[0:T, :]).then_inc(st_y, 16)
                    sp.wait_ge(kiT_c, b + 1)
                    sp.dma_start(kT_d[:, r0:r0 + T], kiT[:, 0, 0:T]).then_inc(st_ki, 16)
                    sp.dma_start(ikT_d[:, r0:r0 + T], kiT[:, 1, 0:T]).then_inc(st_ki, 16)
                    sp.wait_ge(dve_read, len(DVE_G) * (b + 1))
                    sp.dma_start(y_d[b, 0:T, 0:512], ga[0:T, :]).then_inc(st_y, 16)
                    sp.wait_ge(aqT_c, b + 1)
                    sp.dma_start(qT_d[b, :, 0:4 * T], qT[:, :, 0:T]).then_inc(st_q, 16)
                sp.wait_ge(sh_ok, 2 * NBLK)
                for j in range(4):
                    sp.dma_start(hg_s[l, j, :, :], S2[64 * (j % 2):64 * (j % 2) + 64, j // 2, 64 * (j % 2):64 * (j % 2) + 64]).then_inc(st_st, 16)
                    sp.dma_start(rt_s[l, j, :, :], R2[64 * (j % 2):64 * (j % 2) + 64, j // 2, 64 * (j % 2):64 * (j % 2) + 64]).then_inc(st_st, 16)
                sp.wait_ge(st_st, 16 * 16)
                sp.wait_ge(st_q, 16 * NBLK)
                sp.wait_ge(st_iq, 16 * NBLK)
                sp.wait_ge(st_ki, 32 * NBLK)
                sp.wait_ge(st_k, 32 * NBLK)
                sp.wait_ge(st_v, 32 * NBLK)
                sp.wait_ge(st_y, 48 * NBLK)

            @block.tensor
            def _(pe):
                mm = nc.tensor.matmul

                def transposes(dst, src, T):
                    for c, s in enumerate(src):
                        last = nc.tensor.transpose(dst[:, c, 0:T], s, ident[0:T, 0:T])
                    return last

                def x_transposes(t):
                    pe.wait_ge(h_ok, t + 1)
                    for half in range(2):
                        bank = 1 - half
                        if half == 0:
                            wait(pe, iqT_c, t)
                        else:
                            wait(pe, kiT_c, t)
                        for c in range(4):
                            k = 4 * half + c
                            last = nc.tensor.transpose(trv[bank][:, c, :], x[:, k * P:(k + 1) * P], ident[:])
                        last.then_inc(xT_ok, 1)

                def project(t, T, n):
                    g = GI[n]
                    wd = GROUPS[g][1]
                    if not isinstance(t, int) or t > 0 or g >= PJ_BANKS:
                        pn = GROUPS[(g - PJ_BANKS) % NG][0]
                        tt = t if g >= PJ_BANKS else t - 1
                        if pn in ACT_G:
                            pe.wait_ge(act_read, tt * len(ACT_G) + ACT_G[pn])
                        if pn in DVE_G:
                            pe.wait_ge(dve_read, tt * len(DVE_G) + DVE_G[pn])
                    if isinstance(t, int) and t == 0:
                        pe.wait_ge(w_in_s[g], 16)
                    wg = w[:, DC * GOFF[n]:DC * (GOFF[n] + wd)].rearrange("p (c n) -> p c n", c=DC)
                    for c in range(DC):
                        last = mm(PJ[g % PJ_BANKS][0:T, 0:wd], hT[:, c, 0:T], wg[:, c, :],
                                  start=(c == 0), stop=(c == DC - 1))
                    last.then_inc(proj, 1)

                def block_of(t, T):
                    pe.wait_ge(hT_ok, 2 * t + 2)
                    project(t, T, "bqf")
                    project(t, T, "big")
                    pe.wait_ge(act_read, t * len(ACT_G) + ACT_G["bqf"])
                    wait(pe, hT_ok, 2 * t + 2)
                    transposes(trv[0], [bqf[0:T, c, :] for c in range(4)], T).then_inc(bqfT_ok, 1)
                    project(t, T, "cqk")
                    project(t, T, "cvg")
                    pe.wait_ge(rpc_ok, t + 1)
                    wait(pe, aqT_c, t)
                    transposes(trv[1], [rpc[0:T, c * P:(c + 1) * P] for c in range(4)], T).then_inc(cqkT_ok, 1)
                    pe.wait_ge(hq_ok, t + 1)
                    pe.wait_ge(bq_copied, t + 1)
                    pe.wait_ge(f_ok, t + 1)
                    for p in range(2):
                        last = nc.tensor.transpose(TR[0][0:T, p * P:(p + 1) * P], k2T[:, p, 0:T], ident[:])
                    last.then_inc(k2t_ok, 1)
                    for h in (0, 2, 1, 3):
                        p, r = h // 2, slice(64 * (h % 2), 64 * (h % 2) + 64)
                        if h == 1:
                            last.then_inc(even_heads, 1)
                            pe.wait_ge(even_heads, 2 * t + 1)
                        for i in reversed(range(T // WIN)):
                            m = (WIN, 2 * WIN, P, P)[i]
                            q = qe if i == 0 else qw
                            last = mm(ATT[0:m, h * P + i * WIN:h * P + (i + 1) * WIN], kt[r, p, i, 0:m],
                                      q[r, p, i * WIN:(i + 1) * WIN], start=True, stop=True)
                    last.then_inc(atth_ok, 1)
                    project(t, T, "iq")
                    pe.wait_ge(atth_m, t + 1)
                    pe.wait_ge(k2_ok, t + 1)
                    wait(pe, sh_ok, 2 * t)
                    if isinstance(t, int) and t == NB:
                        pe.wait_ge(states_in, 8 * 16)
                    recurrence(T, qe, S2, atth, bi, k2, oh_ok)
                    project(t, T, "kvi")
                    pe.wait_ge(cqkT_c, t + 1)
                    pe.wait_ge(cqs_ok, t + 1)
                    for h in (0, 2, 1, 3):
                        p, r = h // 2, slice(64 * (h % 2), 64 * (h % 2) + 64)
                        if h == 1:
                            last.then_inc(even_heads, 1)
                            pe.wait_ge(even_heads, 2 * t + 2)
                        last = mm(ATT[0:T, h * P:h * P + T], cqkT[r, 2 + p, 0:T], cqkT[r, p, 0:T], start=True, stop=True)
                    last.then_inc(attr_ok, 1)
                    pe.wait_ge(rpi_ok, t + 1)
                    transposes(trv[1], [rpi[0:T, c * P:(c + 1) * P] for c in range(4)], T).then_inc(iqT_ok, 1)
                    pe.wait_ge(attr_m, t + 1)
                    pe.wait_ge(sh_ok, 2 * t + 1)
                    pe.wait_ge(yb_ok, 2 * t + 1)
                    recurrence(T, cqs, R2, attr, cv, cks, or_ok)
                    project(t, T, "aq")
                    pe.wait_ge(ki_ok, t + 1)
                    for c, s in enumerate((ak, ik2)):
                        last = nc.tensor.transpose(trv[0][:, c, 0:T], s[0:T, :], ident[0:T, 0:T])
                    last.then_inc(kiT_ok, 1)
                    project(t, T, "ag")
                    if T == P:
                        x_transposes(t + 1)
                    else:
                        pe.wait_ge(iqT_c, t + 1)
                    pe.wait_ge(aq_ok, t + 1)
                    if T == P:
                        pe.wait_ge(hT_ok, 2 * t + 3)
                    transposes(trv[1], [aq[0:T, c * P:(c + 1) * P] for c in range(4)], T).then_inc(aqT_ok, 1)

                def recurrence(T, q, state, att, v, kend, done):
                    for p in range(2):
                        mm(OU[0:T, p * P:(p + 1) * P], q[:, p, 0:T], state[:, p, :], start=(p == 0), stop=False)
                    for h in range(4):
                        mm(OU[0:T, h * HD:(h + 1) * HD], att[0:T, h, 0:T], v[0:T, h * HD:(h + 1) * HD],
                           start=False, stop=(h == 3))
                    for p in range(2):
                        ke = kend[0:T, p, :] if len(kend.shape) == 3 else kend[0:T, p * P:(p + 1) * P]
                        last = mm(OU[:, 256 + p * P:256 + (p + 1) * P], ke, v[0:T, p * P:(p + 1) * P], start=True, stop=True)
                    last.then_inc(done, 1)

                pe.wait_ge(prep, 1)
                x_transposes(0)
                block_of(0, P)
                if NB > 1:
                    with pe.Fori(1, NB) as t:
                        block_of(t, P)
                block_of(NB, TS)

            @block.scalar
            def _(act):
                A = nc.scalar.activation

                def front(t, T):
                    act.wait_ge(x_in, 16 * t + 16)
                    A(junk[0:T, :], x[0:T, :], ACT.Square, accum_out=ssx[0:T, :]).then_inc(x_sq, 1)
                    act.wait_ge(x_rs, t + 1)
                    A(x[0:T, :], x[0:T, :], ACT.Copy, scale=rsx[0:T, 0:1]).then_inc(h_ok, 1)

                def read_proj(t, n):
                    act.wait_ge(proj, t * NG + GI[n] + 1)

                def block_of(t, T):
                    pj = {n: PJ[GI[n] % PJ_BANKS] for n in GI}
                    read_proj(t, "bqf")
                    wait(act, bqfT_ok, t)
                    A(bqf[0:T, :, :], pj["bqf"][0:T, :].rearrange("p (c n) -> p c n", c=4), ACT.Copy).then_inc(act_read, 1)
                    read_proj(t, "big")
                    wait(act, oh_ok, t)
                    A(bi[0:T, :], pj["big"][0:T, 0:256], ACT.Copy)
                    wait(act, yb_ok, 2 * t)
                    A(egb[0:T, :], pj["big"][0:T, 256:512], ACT.Exp, scale=-1.0).then_inc(act_read, 1)
                    act.wait_ge(bqfT_ok, t + 1)
                    A(ef[:, :, 0:T], trv[0][:, 2:4, 0:T], ACT.Exp, scale=-1.0).then_inc(ef_ok, 1)
                    A(bqT[:, :, 0:T], trv[0][:, 0:2, 0:T], ACT.Copy).then_inc(bq_copied, 1)
                    act.wait_ge(f_ok, t + 1)
                    A(fT[:, :, 0:T], fT[:, :, 0:T], ACT.Ln).then_inc(lf_ok, 1)
                    act.wait_ge(b_ok, t + 1)
                    wait(act, kt_ok, t)
                    wait(act, atth_ok, t)
                    A(qe[:, :, 0:T], bT[:, :, 0:T], ACT.Exp).then_inc(eb_ok, 1)
                    if T > WIN:
                        A(qw[:, :, WIN:T], bw[:, :, WIN:T], ACT.Exp).then_inc(eb_ok, 1)
                    else:
                        A(qw[:, :, 0:T], bT[:, :, 0:T], ACT.Exp).then_inc(eb_ok, 1)
                    for p in range(2):
                        A(k2T[:, p, 0:T], bT[:, p, 0:T], ACT.Exp, scale=-1.0, bias=bT[:, p, T - 1:T])
                        for i in range(T // WIN):
                            ref = 0.0 if i == 0 else bT[:, p, i * WIN - 1:i * WIN]
                            A(kt[:, p, i, 0:(i + 1) * WIN], bT[:, p, 0:(i + 1) * WIN], ACT.Exp, scale=-1.0, bias=ref)
                    A(elast[:], bT[:, :, T - 1], ACT.Exp).then_inc(kt_ok, 1)
                    read_proj(t, "cvg")
                    wait(act, or_ok, t)
                    A(cv[0:T, :], pj["cvg"][0:T, 0:256], ACT.Copy)
                    wait(act, yb_ok, 2 * t)
                    A(egc[0:T, :], pj["cvg"][0:T, 256:512], ACT.Exp, scale=-1.0).then_inc(act_read, 1)
                    act.wait_ge(cqkT_ok, t + 1)
                    wait(act, attr_ok, t)
                    A(cqkT[:, :, 0:T], trv[1][:, :, 0:T], ACT.Copy).then_inc(cqkT_c, 1)
                    act.wait_ge(k2t_ok, t + 1)
                    A(k2[0:T, :, :], TR[0][0:T, 0:256].rearrange("p (c n) -> p c n", c=2), ACT.Copy).then_inc(k2_ok, 1)
                    act.wait_ge(oh_ok, t + 1)
                    wait(act, msoh, 2 * t)
                    A(sqo[0:T, :], OU[0:T, 0:256], ACT.Square).then_inc(sqo_ok, 1)
                    read_proj(t, "kvi")
                    kvi = pj["kvi"]
                    wait(act, st_v, 32 * t)
                    A(av[0:T, :], kvi[0:T, 128:256], ACT.Copy)
                    A(iw[0:T, :], kvi[0:T, 320:328], ACT.Copy, scale=IDX_W_SCALE).then_inc(av_ok, 1)
                    wait(act, msk, t)
                    A(sqk[0:T, :], kvi[0:T, 0:128], ACT.Square).then_inc(sqk_ok, 1)
                    act.wait_ge(iqT_ok, t + 1)
                    wait(act, st_iq, 16 * t)
                    A(iqT[:, :, 0:T], trv[1][:, :, 0:T], ACT.Copy).then_inc(iqT_c, 1)
                    act.wait_ge(or_ok, t + 1)
                    act.wait_ge(msoh, 2 * t + 1)
                    A(sqo[0:T, :], OU[0:T, 0:256], ACT.Square).then_inc(sqo_ok, 1)
                    read_proj(t, "aq")
                    act.wait_ge(rpi_ok, t + 1)
                    act.wait_ge(ki_ok, t + 1)
                    A(sqa[0:T, :], pj["aq"][0:T, :], ACT.Square).then_inc(act_read, 1)
                    if T == P:
                        front_next(t)
                    act.wait_ge(kiT_ok, t + 1)
                    wait(act, st_ki, 32 * t)
                    A(kiT[:, :, 0:T], trv[0][:, 0:2, 0:T], ACT.Copy).then_inc(kiT_c, 1)
                    read_proj(t, "ag")
                    wait(act, dve_read, t * len(DVE_G))
                    A(ega[0:T, :], pj["ag"][0:T, :], ACT.Exp, scale=-1.0).then_inc(act_read, 1)
                    act.wait_ge(aqT_ok, t + 1)
                    wait(act, st_q, 16 * t)
                    A(qT[:, :, 0:T], trv[1][:, :, 0:T], ACT.Copy).then_inc(aqT_c, 1)

                def front_next(t):
                    front(t + 1, P)

                act.wait_ge(prep, 1)
                front(0, P)
                block_of(0, P)
                if NB > 1:
                    with act.Fori(1, NB) as t:
                        block_of(t, P)
                block_of(NB, TS)

            @block.gpsimd
            def _(pool):
                def rsqrt(src_ok, done, out, in_, value):
                    pool.wait_ge(src_ok, value)
                    nc.gpsimd.tensor_tensor(out, in_, mhalf[0:in_.shape[0], 0:in_.shape[1]], ALU.pow).then_inc(done, 1)

                def block_of(t, T):
                    rsqrt(msoh, rsoh, rso[0:T, 0, :], sso[0:T, 0, :], 2 * t + 1)
                    rsqrt(msk, rsk_ok, rsk[0:T, :], ssk[0:T, :], t + 1)
                    rsqrt(msoh, rsoh, rso[0:T, 1, :], sso[0:T, 1, :], 2 * t + 2)
                    rsqrt(msa, rsa_ok, rsa[0:T, :], ssa[0:T, :], t + 1)
                    if T == P:
                        rsqrt(x_ms, x_rs, rsx[:], ssx[:], t + 2)

                pool.wait_ge(prep, 1)
                rsqrt(x_ms, x_rs, rsx[:], ssx[:], 1)
                block_of(0, P)
                if NB > 1:
                    with pool.Fori(1, NB) as t:
                        block_of(t, P)
                block_of(NB, TS)

            @block.vector
            def _(dve):
                V = nc.vector

                def bc(ap, shape, axis):
                    return ap.unsqueeze(axis).broadcast_to(shape)

                def mean_square(step, ss, sq, n, done, width=HD):
                    step(V.tensor_reduce(ss, sq.rearrange("p (h d) -> p h d", h=n), AX_X, ALU.add))
                    V.tensor_scalar(ss, ss, 1.0 / width, EPS, ALU.mult, ALU.add).then_inc(done, 1)

                def rotate(step, t, T, src, dst, nh, read=(), done=()):
                    cos, sin = rope[0:T, t, 0:HALF], rope[0:T, t, HALF:HD]
                    s3 = src.rearrange("p (g d) -> p g d", d=HALF)
                    s4 = src.rearrange("p (h g d) -> p h g d", g=2, d=HALF)
                    d4 = dst.rearrange("p (h g d) -> p h g d", g=2, d=HALF)
                    a, b = rt1[0:T, 0:nh * HD], rt2[0:T, 0:nh * HD]
                    a3 = a.rearrange("p (g d) -> p g d", d=HALF)
                    a4 = a.rearrange("p (h g d) -> p h g d", g=2, d=HALF)
                    b4 = b.rearrange("p (h g d) -> p h g d", g=2, d=HALF)
                    step(V.tensor_tensor(a3, s3, bc(cos, [T, 2 * nh, HALF], 1), ALU.mult))
                    step(V.tensor_tensor(b4[:, :, 0, :], s4[:, :, 1, :], bc(sin, [T, nh, HALF], 1), ALU.mult))
                    step(V.tensor_tensor(b4[:, :, 1, :], s4[:, :, 0, :], bc(sin, [T, nh, HALF], 1), ALU.mult), *read)
                    step(V.tensor_tensor(d4[:, :, 0, :], a4[:, :, 0, :], b4[:, :, 0, :], ALU.subtract))
                    step(V.tensor_tensor(d4[:, :, 1, :], a4[:, :, 1, :], b4[:, :, 1, :], ALU.add), *done)

                def silu(step, out, e, x):
                    step(V.tensor_scalar(e, e, 1.0, None, ALU.add))
                    step(V.reciprocal(e, e))
                    step(V.tensor_tensor(out, e, x, ALU.mult))

                def state_update(step, state, decay, done, value):
                    u = OU[:, 256:512].rearrange("p (c n) -> p c n", c=2)
                    ut3 = ut[:].rearrange("p (c n) -> p c n", c=2)
                    step(V.tensor_tensor(ut3, u, bc(bmask[:], [P, 2, P], 1), ALU.mult))
                    for p in range(2):
                        step(V.scalar_tensor_tensor(out=state[:, p, :], in0=state[:, p, :], scalar=decay[:, p:p + 1],
                                                    in1=ut3[:, p, :], op0=ALU.mult, op1=ALU.add),
                             *((done, value) if p == 1 else ()))

                def block_of(t, T):
                    base = t * DVE_STEPS if isinstance(t, int) else dve.snap(t * DVE_STEPS)
                    n = [0]

                    def step(ins, done=None, value=None):
                        if done is not None:
                            ins.then_inc(done, 1)
                            dve.wait_ge(done, value)
                            return
                        n[0] += 1
                        ins.then_inc(dve_step, 1)
                        dve.wait_ge(dve_step, base + n[0])

                    def was_read(group):
                        return dve_read, t * len(DVE_G) + DVE_G[group]

                    kind = 0 if T == P else 1
                    nw = T // WIN
                    pj = {g: PJ[GI[g] % PJ_BANKS] for g in GI}

                    def read_proj(g):
                        dve.wait_ge(proj, t * NG + GI[g] + 1)

                    dve.wait_ge(ef_ok, t + 1)
                    fv = fT[:, :, 0:T]
                    step(V.tensor_scalar(ef[:, :, 0:T], ef[:, :, 0:T], 1.0, None, ALU.add))
                    step(V.reciprocal(ef[:, :, 0:T], ef[:, :, 0:T]))
                    for p in range(2):
                        step(V.tensor_scalar(fT[:, p, 0:T], ef[:, p, 0:T], lbl[:, 1, p:p + 1], lbl[:, 0, p:p + 1],
                                             ALU.mult, ALU.add))
                    dve.wait_ge(bq_copied, t + 1)
                    step(V.tensor_scalar(kkT[:, :, 0:T], fv, -1.0, 1.0, ALU.mult, ALU.add), f_ok, t + 1)
                    dve.wait_ge(act_read, t * len(ACT_G) + ACT_G["big"])
                    step(V.tensor_scalar(egb[0:T, :], egb[0:T, :], 1.0, None, ALU.add))
                    step(V.reciprocal(egb[0:T, :], egb[0:T, :]))
                    step(V.tensor_tensor(gb[0:T, :], egb[0:T, :], pj["big"][0:T, 256:512], ALU.mult), *was_read("big"))
                    h3 = [T, 4, HD]
                    gb3, gc3 = (g[0:T, :].rearrange("p (h d) -> p h d", h=4) for g in (gb, gc))
                    step(V.tensor_tensor(gb3, gb3, bc(hg[0:T, :], h3, 1), ALU.mult))
                    dve.wait_ge(lf_ok, t + 1)
                    for p in range(2):
                        step(V.tensor_tensor_scan(bT[:, p, 0:T], ones[:, 0:T], fT[:, p, 0:T], 0.0, ALU.mult, ALU.add),
                             *((b_ok, t + 1) if nw == 1 and p == 1 else ()))
                    for p in range(2):
                        if nw > 1:
                            step(V.tensor_tensor(bw[:, p, WIN:T].rearrange("p (w s) -> p w s", s=WIN),
                                                 bT[:, p, WIN:T].rearrange("p (w s) -> p w s", s=WIN),
                                                 bT[:, p, WIN - 1:T - 1:WIN].unsqueeze(2).broadcast_to([P, nw - 1, WIN]),
                                                 ALU.subtract), *((b_ok, t + 1) if p == 1 else ()))
                    dve.wait_ge(eb_ok, 2 * t + 2)
                    step(V.tensor_tensor(qe[:, :, 0:T], qe[:, :, 0:T], bqT[:, :, 0:T], ALU.mult))
                    if nw > 1:
                        step(V.tensor_tensor(qw[:, :, WIN:T], qw[:, :, WIN:T], bqT[:, :, WIN:T], ALU.mult))
                    dve.wait_ge(kt_ok, t + 1)
                    for p in range(2):
                        step(V.tensor_tensor(kt[:, p, 0:nw, 0:T], kt[:, p, 0:nw, 0:T],
                                             bc(kkT[:, p, 0:T], [P, nw, T], 1), ALU.mult))
                    step(V.tensor_tensor(k2T[:, :, 0:T], k2T[:, :, 0:T], kkT[:, :, 0:T], ALU.mult), hq_ok, t + 1)
                    read_proj("cqk")
                    wait(dve, cqkT_ok, t)
                    wait(dve, or_ok, t)
                    rotate(step, t, T, pj["cqk"][0:T, :], rpc[0:T, :], 8, was_read("cqk"))
                    step(V.tensor_tensor(cks[0:T, :].rearrange("p (h d) -> p h d", h=4),
                                         rpc[0:T, 256:512].rearrange("p (h d) -> p h d", h=4),
                                         ksc[0:T, kind, :].unsqueeze(2).broadcast_to(h3), ALU.mult), rpc_ok, t + 1)
                    dve.wait_ge(act_read, t * len(ACT_G) + ACT_G["cvg"])
                    step(V.tensor_scalar(egc[0:T, :], egc[0:T, :], 1.0, None, ALU.add))
                    step(V.reciprocal(egc[0:T, :], egc[0:T, :]))
                    step(V.tensor_tensor(gc[0:T, :], egc[0:T, :], pj["cvg"][0:T, 256:512], ALU.mult), *was_read("cvg"))
                    step(V.tensor_tensor(gc3, gc3, bc(rg[0:T, :], h3, 1), ALU.mult))
                    dve.wait_ge(cqkT_c, t + 1)
                    step(V.tensor_tensor(cqs[:, :, 0:T], trv[1][:, 0:2, 0:T], lrow[:, :, 0:T], ALU.mult), cqs_ok, t + 1)
                    dve.wait_ge(atth_ok, t + 1)
                    attp = ATT[:].rearrange("p (h t) -> p h t", h=4)
                    for i in range(nw):
                        m = (i + 1) * WIN
                        tw = slice(i * WIN, m)
                        step(V.tensor_tensor(atth[0:m, :, tw], attp[0:m, :, tw], bc(causal[0:m, tw], [m, 4, WIN], 1), ALU.mult),
                             *((atth_m, t + 1) if i == nw - 1 else ()))
                    read_proj("iq")
                    wait(dve, iqT_ok, t)
                    rotate(step, t, T, pj["iq"][0:T, :], rpi[0:T, :], 8, was_read("iq"), (rpi_ok, t + 1))

                    def mixer_out(j, state, decay, y, gate):
                        dve.wait_ge(sqo_ok, 2 * t + 1 + j)
                        mean_square(step, sso[0:T, j, :], sqo[0:T, :], 4, msoh)
                        state_update(step, state, decay, sh_ok, 2 * t + 1 + j)
                        dve.wait_ge(rsoh, 2 * t + 1 + j)
                        wait(dve, st_y, 48 * t)
                        y3 = y[0:T, :].rearrange("p (h d) -> p h d", h=4)
                        o3 = OU[0:T, 0:256].rearrange("p (h d) -> p h d", h=4)
                        step(V.tensor_tensor(y3, o3, rso[0:T, j, :].unsqueeze(2).broadcast_to(h3), ALU.mult))
                        step(V.tensor_tensor(y[0:T, :], y[0:T, :], gate[0:T, :], ALU.mult), yb_ok, 2 * t + 1 + j)

                    mixer_out(0, S2, elast, yb, gb)
                    dve.wait_ge(attr_ok, t + 1)
                    step(V.tensor_tensor(attr[0:T, :, 0:T], attp[0:T, :, 0:T], dmat[0:T, :, 0:T], ALU.mult), attr_m, t + 1)
                    kvi = pj["kvi"]
                    read_proj("kvi")
                    dve.wait_ge(sqk_ok, t + 1)
                    mean_square(step, ssk[0:T, :], sqk[0:T, :], 2, msk)
                    wait(dve, kiT_ok, t)
                    wait(dve, st_k, 32 * t)
                    rotate(step, t, T, kvi[0:T, 256:320], ik2[0:T, 0:HD], 1)
                    step(V.tensor_copy(ik2[0:T, HD:P], ik2[0:T, 0:HD]))
                    dve.wait_ge(rsk_ok, t + 1)
                    k3 = sqk[0:T, :].rearrange("p (h d) -> p h d", h=2)
                    step(V.tensor_tensor(k3, kvi[0:T, 0:P].rearrange("p (h d) -> p h d", h=2),
                                         rsk[0:T, :].unsqueeze(2).broadcast_to([T, 2, HD]), ALU.mult), *was_read("kvi"))
                    step(V.tensor_tensor(k3, k3, bc(kg[0:T, :], [T, 2, HD], 1), ALU.mult))
                    rotate(step, t, T, sqk[0:T, :], ak[0:T, :], 2, (), (ki_ok, t + 1))
                    dve.wait_ge(or_ok, t + 1)
                    mixer_out(1, R2, gt[:, kind, :], yc, gc)
                    dve.wait_ge(act_read, t * len(ACT_G) + ACT_G["aq"])
                    mean_square(step, ssa[0:T, :], sqa[0:T, :], 8, msa)
                    dve.wait_ge(rsa_ok, t + 1)
                    a3 = sqa[0:T, :].rearrange("p (h d) -> p h d", h=8)
                    step(V.tensor_tensor(a3, pj["aq"][0:T, :].rearrange("p (h d) -> p h d", h=8),
                                         rsa[0:T, :].unsqueeze(2).broadcast_to([T, 8, HD]), ALU.mult), *was_read("aq"))
                    step(V.tensor_tensor(a3, a3, bc(qg[0:T, :], [T, 8, HD], 1), ALU.mult))
                    wait(dve, aqT_ok, t)
                    rotate(step, t, T, sqa[0:T, :], aq[0:T, :], 8, (), (aq_ok, t + 1))
                    if T == P:
                        x_mean_square(t + 1)
                    dve.wait_ge(act_read, t * len(ACT_G) + ACT_G["ag"])
                    wait(dve, st_y, 48 * t)
                    step(V.tensor_scalar(ega[0:T, :], ega[0:T, :], 1.0, None, ALU.add))
                    step(V.reciprocal(ega[0:T, :], ega[0:T, :]))
                    step(V.tensor_tensor(ga[0:T, :], ega[0:T, :], pj["ag"][0:T, :], ALU.mult), *was_read("ag"))
                    if T == P:
                        x_to_hT(t + 1)
                        assert n[0] == DVE_STEPS, n[0]

                def x_mean_square(t):
                    dve.wait_ge(x_sq, t + 1)
                    V.tensor_scalar(ssx[:], ssx[:], 1.0 / D, EPS, ALU.mult, ALU.add).then_inc(x_ms, 1)

                def x_to_hT(t):
                    for half in range(2):
                        dve.wait_ge(xT_ok, 2 * t + half + 1)
                        V.tensor_tensor(hT[:, 4 * half:4 * half + 4, :], trv[1 - half],
                                        ng[:, 4 * half:4 * half + 4].unsqueeze(2).broadcast_to([P, 4, P]),
                                        ALU.mult).then_inc(hT_ok, 1)

                V.memset(mhalf[:], -0.5)
                V.memset(ones[:], 1.0)
                V.memset(kt[:], 0.0)
                V.memset(atth[:], 0.0)
                V.memset(S2[:], 0.0)
                dve.wait_ge(consts, 16 * 12)
                V.tensor_copy(lbl[:, 0, :], lbt[:, l, :])
                V.tensor_copy(lbl[:, 1, :], oml[:, l, :])
                V.memset(R2[:], 0.0).then_inc(prep, 1)
                dve.wait_ge(prep, 1)
                x_mean_square(0)
                x_to_hT(0)
                block_of(0, P)
                if NB > 1:
                    with dve.Fori(1, NB) as t:
                        block_of(t, P)
                block_of(NB, TS)

    def attention_half(l, sem):
        with ExitStack() as ctx:
            def sb(name, shape, dt=F32):
                return ctx.enter_context(nc.sbuf_tensor(name, shape, dt))

            wo = sb("w_out_sb", [P, DC, D])
            kT = [sb("kT_p", [P, SEQ]), sb("kT_s", [P, PAST + TS])]
            kTb = [sb("kTb_p", [P, SEQ], BF16), sb("kTb_s", [P, PAST + TS], BF16)]
            ikT = [sb("ikT_p", [P, SEQ]), sb("ikT_s", [P, PAST + TS])]
            va = [sb("va_p", [P, NB, 2, P]), sb("va_s", [P, NPB + 1, 2, P])]
            identb = sb("identb", [P, 4, P], BF16)
            onesb = sb("onesb", [P, P], BF16)
            pw = sb("pw", [P, NIT + 1])
            WMAX = max(SEQ, PAST + TS)
            sc = [sb("sc0", [P, WMAX]), sb("sc1", [P, WMAX])]
            rl = sb("rl", [P, 4, 512])
            mneg = [sb("mneg0", [P, WMAX], BF16), sb("mneg1", [P, WMAX], BF16)]
            glo, ghi = sb("glo", [P, WMAX], BF16), sb("ghi", [P, WMAX], BF16)
            junk = sb("junkb", [P, 512], BF16)
            iqT, iw = sb("iqTb", [P, 2, 4 * P]), sb("iwb", [P, 2, 8])
            qT, qTb = sb("qTf", [P, 2, 4 * P]), sb("qTh", [P, 2, 4 * P], BF16)
            yt, xr = sb("yt", [P, 2, D]), sb("xr", [P, 2, D])
            pt = sb("pt", [P, 4, 512])
            oT = sb("oT", [P, 2, 512])
            yT = sb("yTb", [P, DC, P])
            on, rs = sb("on", [P, 512]), sb("rs", [P, 8])
            mxt, mx = sb("mxt", [P, 8, 5]), sb("mx", [P, 8])
            md = sb("md", [P, 8, P], BF16)
            small = {n: sb(n, [P, 1]) for n in "vmax vmin rng mid cnt dlt lo hi chi need".split()}
            stp = sb("stp", [P, NIT + 1])

            SC = [[ctx.enter_context(nc.psum_tensor(f"SC{h}{i}", [P, 512], F32)) for i in range(2)] for h in range(2)]
            PV = [ctx.enter_context(nc.psum_tensor(f"PV{i}", [P, 512], F32)) for i in range(2)]
            X = [ctx.enter_context(nc.psum_tensor(f"X{i}", [P, 512], F32)) for i in range(2)]

            names = ("b_wo b_kp b_ks b_vp b_vs b_const b_prep kb_ok b_iq0 b_iq1 b_q0 b_q1 b_y0 b_y1 b_x0 b_x1 b_st0 b_st1 "
                     "idx_ok relu_ok acc_ok qk_ok max_ok qkt_ok exp_ok pv_ok oT_ok oX_ok on_ok yX_ok yT_ok op_ok "
                     "res_ok md_ok mx_ok mneg_ok qb_ok b_step x_read")
            s = {n: sem(n) for n in names.split()}

            def keys_of(b):
                return (0, (b + 1) * P, K_P) if b < NB else (1, PAST + TS, K_S)

            def searched(b):
                _, W, K = keys_of(b)
                return W > K

            def tiles(W):
                return [(c, min(512, W - c)) for c in range(0, W, 512)]

            def key_blocks(W):
                return [(c, min(P, W - c)) for c in range(0, W, P)]

            def idx_load(b):
                return sum(searched(i) for i in range(b % 2, b + 1, 2))

            def before(b, f):
                return sum(f(i) for i in range(b))

            def n_idx(b):
                return 8 * len(tiles(keys_of(b)[1])) if searched(b) else 0

            def n_qk(b):
                return 8 * len(tiles(keys_of(b)[1]))

            def n_main(b):
                return 2 * len(key_blocks(keys_of(b)[1]))

            block = ctx.enter_context(nc.Block())

            @block.sync
            def _(sp):
                def go(d, src, name):
                    sp.dma_start(d, src).then_inc(s[name], 16)

                def load_idx(b):
                    r0, T = rows(b)
                    if not searched(b):
                        return
                    if b >= 2 and searched(b - 2):
                        sp.wait_ge(s["idx_ok"], before(b - 1, n_idx))
                        sp.wait_ge(s["acc_ok"], before(b - 1, n_idx))
                    go(iqT[:, b % 2, 0:4 * T], iqT_d[b, :, 0:4 * T], f"b_iq{b % 2}")
                    go(iw[0:T, b % 2, :], iw_d[b, 0:T, :], f"b_iq{b % 2}")

                def load_q(b):
                    r0, T = rows(b)
                    if b >= 2:
                        sp.wait_ge(s["qkt_ok"], before(b - 1, n_main))
                        sp.wait_ge(s["qb_ok"], b - 1)
                        sp.wait_ge(s["yX_ok"], b - 1)
                    go(qT[:, b % 2, 0:4 * T], qT_d[b, :, 0:4 * T], f"b_q{b % 2}")
                    go(yt[0:T, b % 2, :], y_d[b, 0:T, :], f"b_y{b % 2}")
                    if b >= 2:
                        sp.wait_ge(s[f"b_st{b % 2}"], 16 * (b // 2))
                    go(xr[0:T, b % 2, :], xs[l, r0:r0 + T, :], f"b_x{b % 2}")

                load_idx(0)
                load_q(0)
                go(kT[0][:], kT_d[:, 0:SEQ], "b_kp")
                go(ikT[0][:], ikT_d[:, 0:SEQ], "b_kp")
                for h in range(2):
                    go(va[0][:, :, h, 0:HD], v_p[l, :, h * HD:(h + 1) * HD].rearrange("(b p) d -> p b d", p=P), "b_vp")
                go(pw[:], c_pow[:, :], "b_const")
                load_idx(1)
                load_q(1)
                go(wo[:], w_out[l, :, :, :], "b_wo")
                go(kT[1][:, PAST:PAST + TS], kT_d[:, SEQ:SEQ + TS], "b_ks")
                go(ikT[1][:, PAST:PAST + TS], ikT_d[:, SEQ:SEQ + TS], "b_ks")
                for h in range(2):
                    go(va[1][:, 0:NPB, h, 0:HD], cache_v[l, :, :, h * HD:(h + 1) * HD], "b_vs")
                    go(va[1][0:TS, NPB, h, 0:HD], v_s[l, :, h * HD:(h + 1) * HD], "b_vs")
                go(kT[1][:, 0:PAST], cache_k[l, :, :], "b_ks")
                for h in range(2):
                    go(ikT[1][h * HD:(h + 1) * HD, 0:PAST], cache_i[l, :, :], "b_ks")
                for b in range(NBLK):
                    r0, T = rows(b)
                    if b + 2 < NBLK:
                        load_idx(b + 2)
                    if b >= 1:
                        q0, Tq = rows(b - 1)
                        sp.wait_ge(s["res_ok"], 2 * b)
                        go(xs[l + 1, q0:q0 + Tq, :], xr[0:Tq, (b - 1) % 2, :], f"b_st{(b - 1) % 2}")
                    if 2 <= b + 1 < NBLK:
                        load_q(b + 1)
                sp.wait_ge(s["res_ok"], 2 * NBLK)
                go(xs[l + 1, r0:r0 + T, :], xr[0:T, (NBLK - 1) % 2, :], f"b_st{(NBLK - 1) % 2}")
                sp.wait_ge(s["b_st0"], 16 * ((NBLK + 1) // 2))
                sp.wait_ge(s["b_st1"], 16 * (NBLK // 2))

            @block.tensor
            def _(pe):
                mm = nc.tensor.matmul
                uses = [[], []]

                def bank(half, reader):
                    n = len(uses[half])
                    if n >= 2:
                        pe.wait_ge(*uses[half][n - 2])
                    uses[half].append(reader)
                    return SC[half][n % 2]

                def logit_maxima(b):
                    c, W, _ = keys_of(b)
                    T = rows(b)[1]
                    n = before(b, n_qk)
                    pe.wait_ge(s["qb_ok"], b + 1)
                    if b in (0, NB):
                        pe.wait_ge(s["kb_ok"], 1 if b == 0 else 2)
                    for c0, wd in tiles(W):
                        for p in range(4):
                            for half in range(2):
                                r = slice(64 * half, 64 * half + 64)
                                n += 1
                                ps = bank(half, (s["max_ok"], n))
                                mm(ps[0:T, 0:wd], qTb[r, b % 2, p * T:(p + 1) * T], kTb[c][r, c0:c0 + wd],
                                   start=True, stop=True).then_inc(s["qk_ok"], 1)

                def indexer(b):
                    c, W, _ = keys_of(b)
                    T = rows(b)[1]
                    if not searched(b):
                        return
                    n = before(b, n_idx)
                    pe.wait_ge(s[f"b_iq{b % 2}"], 32 * idx_load(b))
                    if b == NB:
                        pe.wait_ge(s["b_ks"], 80)
                    for c0, wd in tiles(W):
                        for p in range(4):
                            for half in range(2):
                                r = slice(64 * half, 64 * half + 64)
                                n += 1
                                ps = bank(half, (s["relu_ok"], n))
                                mm(ps[0:T, 0:wd], iqT[r, b % 2, p * T:(p + 1) * T], ikT[c][r, c0:c0 + wd],
                                   start=True, stop=True).then_inc(s["idx_ok"], 1)

                def attention(b):
                    c, W, _ = keys_of(b)
                    T = rows(b)[1]
                    pe.wait_ge(s["md_ok"], b + 1)
                    pe.wait_ge(s["mneg_ok"], b + 1)
                    if b >= 1:
                        pe.wait_ge(s["oT_ok"], 2 * b)
                    if b == 0:
                        pe.wait_ge(s["b_vp"], 32)
                    if b == NB:
                        pe.wait_ge(s["b_vs"], 64)
                    base = before(b, n_main)
                    steps = [(k0, kw, kv) for k0, kw in key_blocks(W) for kv in range(2)]

                    def logits(i):
                        k0, kw, kv = steps[i]
                        r = slice(64 * kv, 64 * kv + 64)
                        ps = bank(kv, (s["exp_ok"], base + i + 1))
                        mm(ps[0:kw, 0:4 * T], kT[c][r, k0:k0 + kw], qT[r, b % 2, 0:4 * T], start=True, stop=False)
                        mm(ps[0:kw, 0:4 * T], mneg[b % 2][0:T, k0:k0 + kw], identb[0:T, :, 0:T], start=False, stop=False)
                        mm(ps[0:kw, 0:4 * T], onesb[0:T, 0:kw], md[0:T, 4 * kv:4 * kv + 4, 0:T],
                           start=False, stop=True).then_inc(s["qkt_ok"], 1)

                    def values(i):
                        k0, kw, kv = steps[i]
                        pe.wait_ge(s["exp_ok"], base + i + 1)
                        mm(PV[kv][:, 0:4 * T], va[c][0:kw, k0 // P, kv, :], pt[0:kw, (base + i) % 4, 0:4 * T],
                           start=(k0 == 0), stop=(k0 + kw == W)).then_inc(s["pv_ok"], 1)

                    AHEAD = 2
                    for i in range(min(AHEAD, len(steps))):
                        logits(i)
                    for i in range(len(steps)):
                        if i + AHEAD < len(steps):
                            logits(i + AHEAD)
                        values(i)

                def out_transposes(b):
                    T = rows(b)[1]
                    pe.wait_ge(s["oT_ok"], 2 * b + 2)
                    if b >= 1:
                        pe.wait_ge(s["res_ok"], 2 * b)
                    for kv in range(2):
                        for p in range(4):
                            last = nc.tensor.transpose(X[kv][0:T, p * P:(p + 1) * P], oT[:, kv, p * T:(p + 1) * T], ident[:])
                        last.then_inc(s["oX_ok"], 1)

                def mixed_transposes(b):
                    T = rows(b)[1]
                    pe.wait_ge(s["on_ok"], b + 1)
                    for c in range(DC):
                        last = nc.tensor.transpose(X[c // 4][:, (c % 4) * P:(c % 4) * P + T], yt[0:T, b % 2, c * P:(c + 1) * P],
                                                   ident[0:T, 0:T])
                    last.then_inc(s["yX_ok"], 1)

                def project(b):
                    T = rows(b)[1]
                    pe.wait_ge(s["yT_ok"], b + 1)
                    if b == 0:
                        pe.wait_ge(s["b_wo"], 16)
                    for n in range(2):
                        for c in range(DC):
                            last = mm(X[n][0:T, :], yT[:, c, 0:T], wo[:, c, n * 512:(n + 1) * 512],
                                      start=(c == 0), stop=(c == DC - 1))
                        last.then_inc(s["op_ok"], 1)

                pe.wait_ge(s["b_prep"], 1)
                pe.wait_ge(s["b_kp"], 32)
                indexer(0)
                for b in range(NBLK):
                    logit_maxima(b)
                    if b >= 1:
                        out_transposes(b - 1)
                    if b + 1 < NBLK:
                        indexer(b + 1)
                    if b >= 1:
                        mixed_transposes(b - 1)
                        project(b - 1)
                    attention(b)
                out_transposes(NBLK - 1)
                mixed_transposes(NBLK - 1)
                project(NBLK - 1)

            @block.scalar
            def _(act):
                A = nc.scalar.activation

                def indexer(b):
                    if not searched(b):
                        return
                    T = rows(b)[1]
                    n = before(b, n_idx)
                    for c0, wd in tiles(keys_of(b)[1]):
                        for p in range(4):
                            for half in range(2):
                                n += 1
                                act.wait_ge(s["idx_ok"], n)
                                if n > 4:
                                    act.wait_ge(s["acc_ok"], n - 4)
                                A(rl[0:T, (n - 1) % 4, 0:wd], sc_bank(half)[0:T, 0:wd], ACT.Relu).then_inc(s["relu_ok"], 1)

                count = [0, 0]

                def sc_bank(half):
                    count[half] += 1
                    return SC[half][(count[half] - 1) % 2]

                def skip_maxima(b):
                    for half in range(2):
                        count[half] += n_qk(b) // 2

                def exponentials(b):
                    c, W, _ = keys_of(b)
                    T = rows(b)[1]
                    n = before(b, n_main)
                    for k0, kw in key_blocks(W):
                        for kv in range(2):
                            n += 1
                            act.wait_ge(s["qkt_ok"], n)
                            if n > 4:
                                act.wait_ge(s["pv_ok"], n - 4)
                            A(pt[0:kw, (n - 1) % 4, 0:4 * T], sc_bank(kv)[0:kw, 0:4 * T], ACT.Exp,
                              scale=HD ** -0.5).then_inc(s["exp_ok"], 1)
                    if b >= 1:
                        act.wait_ge(s["oX_ok"], 2 * b)
                    for kv in range(2):
                        act.wait_ge(s["pv_ok"], n - 1 + kv)
                        A(oT[:, kv, 0:4 * T], PV[kv][:, 0:4 * T], ACT.Copy).then_inc(s["oT_ok"], 1)

                def mixed_copies(b):
                    T = rows(b)[1]
                    act.wait_ge(s["yX_ok"], b + 1)
                    if b >= 1:
                        act.wait_ge(s["op_ok"], 2 * b)
                    A(yT[:, 0:4, 0:T], X[0][:].rearrange("p (c t) -> p c t", c=4)[:, :, 0:T], ACT.Copy)
                    A(yT[:, 4:8, 0:T], X[1][:].rearrange("p (c t) -> p c t", c=4)[:, :, 0:T], ACT.Copy).then_inc(s["yT_ok"], 1)

                indexer(0)
                for b in range(NBLK):
                    skip_maxima(b)
                    if b + 1 < NBLK:
                        indexer(b + 1)
                    if b >= 1:
                        mixed_copies(b - 1)
                    exponentials(b)
                mixed_copies(NBLK - 1)

            @block.gpsimd
            def _(pool):
                G = nc.gpsimd
                G.memset(va[0][:, :, :, HD:P], 1.0)
                G.memset(va[1][:, :, :, HD:P], 1.0)
                G.memset(onesb[:], 1.0)
                for i in range(4):
                    last = G.tensor_copy(identb[:, i, :], ident[:])
                last.then_inc(s["b_prep"], 1)
                pool.wait_ge(s["b_prep"], 1)

                def q_copy(b):
                    T = rows(b)[1]
                    pool.wait_ge(s[f"b_q{b % 2}"], 16 * (b // 2 + 1))
                    if b >= 2:
                        pool.wait_ge(s["qk_ok"], before(b - 1, n_qk))
                    G.tensor_copy(qTb[:, b % 2, 0:4 * T], qT[:, b % 2, 0:4 * T]).then_inc(s["qb_ok"], 1)

                def max_diagonals(b):
                    T = rows(b)[1]
                    pool.wait_ge(s["mx_ok"], b + 1)
                    if b >= 1:
                        pool.wait_ge(s["qkt_ok"], before(b, n_main))
                    G.tensor_tensor(md[0:T, :, 0:T], identb[0:T, 0, 0:T].unsqueeze(1).broadcast_to([T, 8, T]),
                                    mx[0:T, :].unsqueeze(2).broadcast_to([T, 8, T]), ALU.mult).then_inc(s["md_ok"], 1)

                pool.wait_ge(s["b_kp"], 32)
                G.tensor_copy(kTb[0][:], kT[0][:]).then_inc(s["kb_ok"], 1)
                q_copy(0)
                pool.wait_ge(s["b_ks"], 80)
                G.tensor_copy(kTb[1][:], kT[1][:]).then_inc(s["kb_ok"], 1)
                q_copy(1)
                for b in range(NBLK):
                    max_diagonals(b)
                    if b + 2 < NBLK:
                        q_copy(b + 2)

            @block.vector
            def _(dve):
                V = nc.vector
                step = Steps(dve, s["b_step"])
                count = [0, 0]

                def sc_bank(half):
                    count[half] += 1
                    return SC[half][(count[half] - 1) % 2]

                def maxima(b):
                    c, W, _ = keys_of(b)
                    T = rows(b)[1]
                    n = before(b, n_qk)
                    nt = len(tiles(W))
                    for j, (c0, wd) in enumerate(tiles(W)):
                        for p in range(4):
                            for half in range(2):
                                n += 1
                                dve.wait_ge(s["qk_ok"], n)
                                h = 4 * half + p
                                if n > 1:
                                    dve.wait_ge(s["max_ok"], n - 1)
                                V.tensor_tensor_reduce(out=junk[0:T, 0:wd], in0=sc_bank(half)[0:T, 0:wd],
                                                       in1=mneg[b % 2][0:T, c0:c0 + wd], scale=1.0, scalar=-3e38,
                                                       op0=ALU.add, op1=ALU.max,
                                                       accum_out=mxt[0:T, h, j:j + 1]).then_inc(s["max_ok"], 1)
                    dve.wait_ge(s["max_ok"], n)
                    if b >= 1:
                        dve.wait_ge(s["md_ok"], b)
                    step(V.tensor_reduce(mx[0:T, :], mxt[0:T, :, 0:nt], AX_X, ALU.max))
                    V.tensor_scalar(mx[0:T, :], mx[0:T, :], -1.0, None, ALU.mult).then_inc(s["mx_ok"], 1)

                def normalise(b):
                    T = rows(b)[1]
                    dve.wait_ge(s[f"b_y{b % 2}"], 16 * (b // 2 + 1))
                    dve.wait_ge(s["oX_ok"], 2 * b + 2)
                    for kv in range(2):
                        x3 = X[kv][0:T, :].rearrange("p (h d) -> p h d", h=4)
                        step(V.reciprocal(rs[0:T, 4 * kv:4 * kv + 4], x3[:, :, HD]))
                        step(V.tensor_tensor(on[0:T, 256 * kv:256 * kv + 256].rearrange("p (h d) -> p h d", h=4),
                                             x3[:, :, 0:HD], rs[0:T, 4 * kv:4 * kv + 4].unsqueeze(2)
                                             .broadcast_to([T, 4, HD]), ALU.mult))
                    V.tensor_tensor(yt[0:T, b % 2, 0:512], yt[0:T, b % 2, 0:512], on[0:T, :], ALU.mult).then_inc(s["on_ok"], 1)

                def accumulate(b):
                    if not searched(b):
                        return
                    T = rows(b)[1]
                    n = before(b, n_idx)
                    for half in range(2):
                        count[half] += n_idx(b) // 2
                    dst = sc[b % 2]
                    dve.wait_ge(s[f"b_iq{b % 2}"], 32 * idx_load(b))
                    for c0, wd in tiles(keys_of(b)[1]):
                        for p in range(4):
                            for half in range(2):
                                n += 1
                                h = 4 * half + p
                                dve.wait_ge(s["relu_ok"], n)
                                src, w1 = rl[0:T, (n - 1) % 4, 0:wd], iw[0:T, b % 2, h:h + 1]
                                o = dst[0:T, c0:c0 + wd]
                                if p == 0 and half == 0:
                                    V.tensor_scalar(o, src, w1, None, ALU.mult).then_inc(s["acc_ok"], 1)
                                else:
                                    dve.wait_ge(s["acc_ok"], n - 1)
                                    V.scalar_tensor_tensor(out=o, in0=src, scalar=w1, in1=o, op0=ALU.mult,
                                                           op1=ALU.add).then_inc(s["acc_ok"], 1)
                    dve.wait_ge(s["acc_ok"], n)

                def add_residual(b):
                    T = rows(b)[1]
                    dve.wait_ge(s[f"b_x{b % 2}"], 16 * (b // 2 + 1))
                    for n in range(2):
                        dve.wait_ge(s["op_ok"], 2 * b + n + 1)
                        o = xr[0:T, b % 2, n * 512:(n + 1) * 512]
                        V.tensor_tensor(o, o, X[n][0:T, :], ALU.add).then_inc(s["res_ok"], 1)

                def select(b):
                    c, W, K = keys_of(b)
                    T = rows(b)[1]
                    out = mneg[b % 2][0:T, 0:W]
                    if b >= 2:
                        dve.wait_ge(s["qkt_ok"], before(b - 1, n_main))
                    if not searched(b):
                        step(V.memset(out, 0.0))
                        V.memset(mneg[b % 2][0:64, W - 64:W], -MASKED).then_inc(s["mneg_ok"], 1)
                        dve.wait_ge(s["mneg_ok"], b + 1)
                        return
                    v = {n: t[0:T, :] for n, t in small.items()}
                    x = sc[b % 2][0:T, 0:W]
                    lo, hi, mid = v["lo"], v["hi"], v["mid"]
                    step(V.tensor_reduce(v["vmax"], x, AX_X, ALU.max))
                    step(V.tensor_reduce(v["vmin"], x, AX_X, ALU.min))
                    step(V.scalar_tensor_tensor(out=v["rng"], in0=v["vmin"], scalar=-1.0, in1=v["vmax"],
                                                op0=ALU.mult, op1=ALU.max))
                    step(V.tensor_scalar(v["rng"], v["rng"], 1e-30, 2.0, ALU.max, ALU.mult))
                    step(V.tensor_scalar(v["rng"].bitcast(I32), v["rng"].bitcast(I32), 0x7F800000, None, ALU.bitwise_and))
                    step(V.tensor_scalar(stp[0:T, :], pw[0:T, :], v["rng"], None, ALU.mult))
                    if b < NB:
                        step(V.memset(sc[b % 2][0:64, W - 64:W], -BIG))
                    step(V.memset(mid, 0.0))
                    for i in range(NIT):
                        step(V.tensor_scalar(glo[0:T, 0:W], x, mid, None, ALU.is_ge, ALU.add, accum_out=v["cnt"]))
                        step(V.tensor_scalar(v["dlt"], v["cnt"], float(K), stp[0:T, i:i + 1], ALU.is_ge, ALU.mult))
                        step(V.scalar_tensor_tensor(out=mid, in0=v["dlt"], scalar=stp[0:T, i + 1:i + 2], in1=mid,
                                                    op0=ALU.subtract, op1=ALU.add))
                    step(V.tensor_tensor(lo, mid, stp[0:T, NIT:NIT + 1], ALU.subtract))
                    step(V.tensor_tensor(hi, mid, stp[0:T, NIT:NIT + 1], ALU.add))
                    step(V.tensor_scalar(glo[0:T, 0:W], x, lo, None, ALU.is_ge))
                    step(V.tensor_scalar(ghi[0:T, 0:W], x, hi, None, ALU.is_ge, ALU.add, accum_out=v["chi"]))
                    step(V.tensor_scalar(v["need"], v["chi"], -1.0, float(K), ALU.mult, ALU.add))
                    step(V.tensor_tensor_scan(x, glo[0:T, 0:W], ghi[0:T, 0:W], 0.0, ALU.add, ALU.subtract))
                    step(V.scalar_tensor_tensor(out=glo[0:T, 0:W], in0=x, scalar=v["need"], in1=glo[0:T, 0:W],
                                                op0=ALU.is_le, op1=ALU.mult))
                    step(V.tensor_tensor(glo[0:T, 0:W], glo[0:T, 0:W], ghi[0:T, 0:W], ALU.max))
                    V.tensor_scalar(out, glo[0:T, 0:W], -1.0, MASKED, ALU.add, ALU.mult).then_inc(s["mneg_ok"], 1)
                    dve.wait_ge(s["mneg_ok"], b + 1)

                def skip_main(b):
                    for half in range(2):
                        count[half] += n_main(b) // 2

                dve.wait_ge(s["b_const"], 16)
                accumulate(0)
                select(0)
                for b in range(NBLK):
                    maxima(b)
                    if b >= 1:
                        normalise(b - 1)
                    if b + 1 < NBLK:
                        accumulate(b + 1)
                    if b >= 1:
                        add_residual(b - 1)
                    skip_main(b)
                    if b + 1 < NBLK:
                        select(b + 1)
                normalise(NBLK - 1)
                add_residual(NBLK - 1)

    with ExitStack() as whole:
        def sem(name):
            return whole.enter_context(nc.semaphore(name))

        ident = whole.enter_context(nc.sbuf_tensor("ident", [P, P], F32))
        oml = whole.enter_context(nc.sbuf_tensor("oml", [P, DEPTH, 2], F32))
        lbt = whole.enter_context(nc.sbuf_tensor("lbt", [P, DEPTH, 2], F32))

        copied, lb_in, lb_step, lb_exp = sem("copied"), sem("lb_in"), sem("lb_step"), sem("lb_exp")
        with ExitStack() as ctx:
            lg = ctx.enter_context(nc.sbuf_tensor("lg", [P, DEPTH, 2], F32))
            mx = ctx.enter_context(nc.sbuf_tensor("lmx", [P, 2], F32))
            block = ctx.enter_context(nc.Block())

            @block.sync
            def _(sp):
                sp.dma_start(lg[:], lb_logits[:, :, :]).then_inc(lb_in, 16)
                sp.dma_start(ident[:], c_ident[:, :]).then_inc(lb_in, 16)
                sp.dma_start(xs[0, :, :], xin[:, :]).then_inc(copied, 16)
                sp.wait_ge(copied, 16)
                sp.wait_ge(lb_in, 32)

            @block.scalar
            def _(act):
                act.wait_ge(lb_exp, 1)
                nc.scalar.activation(lg[:], lg[:], ACT.Exp).then_inc(lb_exp, 1)

            @block.vector
            def _(dve):
                step = Steps(dve, lb_step)
                dve.wait_ge(lb_in, 32)
                step(nc.vector.tensor_copy(mx[:], lg[:, 0, :]))
                for l in range(1, DEPTH):
                    step(nc.vector.tensor_tensor(mx[:], mx[:], lg[:, l, :], ALU.max))
                for l in range(DEPTH):
                    step(nc.vector.tensor_tensor(lg[:, l, :], lg[:, l, :], mx[:], ALU.subtract))
                nc.vector.memset(lbt[:, 0, :], 0.0).then_inc(lb_exp, 1)
                dve.wait_ge(lb_exp, 2)
                step(nc.vector.tensor_copy(mx[:], lg[:, 0, :]))
                for l in range(1, DEPTH):
                    step(nc.vector.tensor_tensor(mx[:], mx[:], lg[:, l, :], ALU.add))
                step(nc.vector.reciprocal(mx[:], mx[:]))
                for l in range(DEPTH):
                    step(nc.vector.tensor_tensor(lg[:, l, :], lg[:, l, :], mx[:], ALU.mult))
                for l in range(1, DEPTH):
                    step(nc.vector.tensor_tensor(lbt[:, l, :], lbt[:, l - 1, :], lg[:, l, :], ALU.add))
                step(nc.vector.tensor_scalar(oml[:], lbt[:], -1.0, 1.0, ALU.mult, ALU.add))

        sems = {}

        def layer_sem(name):
            if name not in sems:
                sems[name] = sem(name)
            return sems[name]

        with nc.Fori(0, DEPTH) as l:
            recurrent_half(l, layer_sem)
            attention_half(l, layer_sem)
            with nc.Block() as block:
                @block.gpsimd
                def _(pool):
                    for s in sems.values():
                        pool.sem_clear(s)


A_WIDTH = A_HEADS * HD


def shape_constants(seq, past, ts):
    nb = seq // P
    half = HD // 2
    pos = np.zeros((nb + 1, P), np.float32)
    pos[:nb] = np.arange(seq, dtype=np.float32).reshape(nb, P)
    pos[nb, :ts] = past + np.arange(ts)
    freq = (10000.0 ** (-np.arange(half, dtype=np.float64) / half)).astype(np.float32)
    ang = (pos[:, :, None] * freq).astype(np.float32).astype(np.float64)
    rope = np.concatenate([np.cos(ang), np.sin(ang)], -1).astype(np.float32).transpose(1, 0, 2)
    lg = np.log(1.0 - np.exp(np.linspace(np.log(1.0 / 32), np.log(1.0 / 512), 4)))
    n = np.arange(P)
    diff = n[None, :] - n[:, None]
    dmat = np.where(diff[:, None, :] >= 0, np.exp(np.maximum(diff, 0)[:, None, :] * lg[None, :, None]), 0.0) * HD ** -0.5
    lrow = np.zeros((P, 2, P))
    ksc = np.zeros((P, 2, 4))
    gt = np.zeros((P, 2, 2))
    for p in range(2):
        for j in range(2):
            r = slice(64 * j, 64 * j + 64)
            lrow[r, p, :] = np.exp((n + 1.0) * lg[2 * p + j])
            for v, T in enumerate((P, ts)):
                gt[r, v, p] = np.exp(T * lg[2 * p + j])
    for v, T in enumerate((P, ts)):
        ksc[:T, v, :] = np.exp((T - 1.0 - n[:T])[:, None] * lg[None, :]) * HD ** -0.5
    bmask = np.kron(np.eye(2), np.ones((64, 64)))
    causal = (diff >= 0)
    return [np.ascontiguousarray(a.astype(np.float32)) for a in
            (rope, np.eye(P), causal, dmat, lrow, ksc, gt, bmask,
             np.broadcast_to(2.0 ** -np.arange(NIT + 1), (P, NIT + 1)))]


def column_order():
    sizes = [("aq", 512), ("ak", 128), ("av", 128), ("ag", 512), ("iq", 512), ("ik", 64), ("iw", 8), ("bq", 256),
             ("bf", 256), ("bi", 256), ("bg", 256), ("cq", 256), ("ck", 256), ("cv", 256), ("cg", 256)]
    at, cols = 0, {}
    for n, wd in sizes:
        cols[n] = np.arange(at, at + wd)
        at += wd
    pairs = [h for p in range(4) for h in (p, p + 4)]
    for n in ("aq", "iq"):
        cols[n] = cols[n].reshape(8, HD)[pairs].ravel()
    parts = {"bqf": "bq bf", "big": "bi bg", "cqk": "cq ck", "cvg": "cv cg", "iq": "iq", "kvi": "ak av ik iw",
             "aq": "aq", "ag": "ag"}
    return np.concatenate([cols[c] for n, _ in GROUPS for c in parts[n].split()])


def kernel(x_prompt, x_sample, cache_k, cache_v, cache_idx_k, state_hgrn, state_ret, norm_g, w_in, q_norm_g,
           k_norm_g, hgrn_lb_logits, hgrn_norm_g, ret_norm_g, w_out):
    import concourse.bacc as _bacc
    from concourse.bass_utils import run_bass_kernel_spmd as _run

    arr = [np.asarray(a) for a in (x_prompt, x_sample, cache_k, cache_v, cache_idx_k, state_hgrn, state_ret, norm_g,
                                   w_in, q_norm_g, k_norm_g, hgrn_lb_logits, hgrn_norm_g, ret_norm_g, w_out)]
    xp, xsm, ck, cv, ci, sh, sr, ng, wi, qg, kg, lb, hg, rg, wo = arr
    depth, d = ng.shape
    seq, ts, past = xp.shape[1], xsm.shape[1], ck.shape[2]

    def over_partitions(g):
        return np.broadcast_to(g[:, None, :], (depth, P, g.shape[1]))

    wi = wi[:, :, column_order()].reshape(depth, d // P, P, N_IN).transpose(0, 2, 1, 3)
    w_cols = np.concatenate([wi[..., GOFF[n]:GOFF[n] + wd].reshape(depth, P, -1) for n, wd in GROUPS], -1)
    ins = [np.concatenate([xp[0], xsm[0]], 0), ck.reshape(depth, past, 2 * HD).transpose(0, 2, 1),
           cv.reshape(depth, past // P, P, 2 * HD).transpose(0, 2, 1, 3), ci[:, 0].transpose(0, 2, 1), sh[:, 0], sr[:, 0], ng.reshape(depth, d // P, P).transpose(0, 2, 1),
           w_cols, over_partitions(qg), over_partitions(kg), lb.reshape(depth, 2, P).transpose(2, 0, 1), over_partitions(hg),
           over_partitions(rg),
           wo.reshape(depth, d // P, P, d).transpose(0, 2, 1, 3)] + shape_constants(seq, past, ts)
    outs = [(depth + 1, seq + ts, d), (depth, seq, 128), (depth, seq, 128), (depth, seq, HD), (depth, 4, HD, HD),
            (depth, 4, HD, HD), (depth, ts, 128), (depth, ts, 128), (depth, ts, HD), (depth, 4, HD, HD),
            (depth, 4, HD, HD)]
    nc = _bacc.Bacc("TRN2", target_bir_lowering=False, num_devices=1)
    arrays, args = {}, []
    for i, a in enumerate(ins):
        a = np.ascontiguousarray(a)
        arrays[f"in_{i}"] = a
        args.append(nc.dram_tensor(f"in_{i}", a.shape, mybir.dt.from_np(a.dtype), kind="ExternalInput").ap())
    for i, shape in enumerate(outs):
        args.append(nc.dram_tensor(f"out_{i}", shape, F32, kind="ExternalOutput").ap())
    build(nc, *args)
    r = _run(nc, [arrays], core_ids=[0]).results[0]
    x, k, v, ik, h, rt, ks, vs, iks, hs, rs = (r[f"out_{i}"] for i in range(len(outs)))
    y = x[depth]
    return (y[None, :seq], y[None, seq:], k.reshape(depth, 1, seq, 2, HD), v.reshape(depth, 1, seq, 2, HD),
            ik.reshape(depth, 1, seq, HD), h[:, None], rt[:, None], ks.reshape(depth, 1, ts, 2, HD),
            vs.reshape(depth, 1, ts, 2, HD), iks.reshape(depth, 1, ts, HD), hs[:, None], rs[:, None])
```

```python
from contextlib import ExitStack

import numpy as np
import concourse.bass as bass
from concourse import mybir

F32 = mybir.dt.float32
BF16 = mybir.dt.bfloat16
F16 = mybir.dt.float16
I32 = mybir.dt.int32
ALU = mybir.AluOpType
ACT = mybir.ActivationFunctionType
AX_X = mybir.AxisListType.X

P = 128
HD = 64
HALF = HD // 2
CHUNK = 64
A_HEADS, KV_HEADS = 8, 2
GRP = A_HEADS // KV_HEADS
EPS = 1e-6
IDX_W_SCALE = (A_HEADS * HD) ** -0.5
WIN = 32
NIT = 24
ACT_COUNTS = 0.45
BIG = 1e30
W_SCALE = 1024.0
UNSCALE = 1.0 / W_SCALE
W_STAGES = 4
MASKED = 30000.0

GROUPS = [("bqf", 512), ("big", 512), ("cqk", 512), ("cvg", 512), ("iq", 512), ("kvi", 328), ("aq", 512), ("ag", 512)]
GI = {n: i for i, (n, _) in enumerate(GROUPS)}
GOFF = {n: sum(w for _, w in GROUPS[:i]) for i, (n, _) in enumerate(GROUPS)}
N_IN = sum(w for _, w in GROUPS)
NG = len(GROUPS)
PJ_BANKS = 4
ACT_G = {"bqf": 1, "big": 2, "cvg": 3, "aq": 4, "ag": 5}
DVE_G = {"big": 1, "cqk": 2, "cvg": 3, "iq": 4, "kvi": 5, "aq": 6, "ag": 7}
DVE_STEPS = 49


class Steps:

    def __init__(self, eng, sem, base=0):
        self.eng, self.sem, self.base, self.n = eng, sem, base, 0

    def __call__(self, ins):
        self.n += 1
        ins.then_inc(self.sem, 1)
        self.eng.wait_ge(self.sem, self.base + self.n)


def build(nc, xin, cache_k, cache_v, cache_i, st_h, st_r, norm_g, w_in, q_g, k_g, lb_logits, h_g, r_g, w_out,
          c_rope, c_ident, c_causal, c_dmat, c_lrow, c_ksc, c_gt, c_bmask, c_pow,
          xs, k_p, v_p, ik_p, hg_p, rt_p, k_s, v_s, ik_s, hg_s, rt_s):
    DEPTH, D = w_in.shape[0], w_out.shape[3]
    DC = D // P
    SEQ = k_p.shape[1]
    TS = k_s.shape[1]
    PAST = cache_k.shape[2]
    NB = SEQ // P
    NPB = PAST // P
    K_P, K_S = min(256, SEQ // 4), min(256, (PAST + TS) // 4)
    NBLK = NB + 1

    def scratch(name, shape):
        return nc.dram_tensor(name, shape, F32, kind="Internal").ap()

    kT_d, ikT_d = scratch("kT_d", [P, SEQ + TS]), scratch("ikT_d", [P, SEQ + TS])
    qT_d, iqT_d = scratch("qT_d", [NBLK, P, 4 * P]), scratch("iqT_d", [NBLK, P, 4 * P])
    iw_d, y_d = scratch("iw_d", [NBLK, P, 8]), scratch("y_d", [NBLK, P, D])

    def rows(b):
        return (b * P, P) if b < NB else (SEQ, TS)

    def recurrent_half(l, sem):
        with ExitStack() as ctx:
            def sb(name, shape, dt=F32):
                return ctx.enter_context(nc.sbuf_tensor(name, shape, dt))

            wh, wl = sb("w_in_hi", [P, DC * N_IN], F16), sb("w_in_lo", [P, DC * N_IN], F16)
            wst = sb("w_stage", [P, W_STAGES, 512])
            rope = sb("rope", [P, NBLK, HD])
            causal = sb("causal", [P, P])
            dmat = sb("dmat", [P, 4, P])
            lrow = sb("lrow", [P, 2, P])
            ksc = sb("ksc", [P, 2, 4])
            gt = sb("gt", [P, 2, 2])
            bmask = sb("bmask", [P, P])
            ng = sb("ng", [P, DC])
            qg, kg = sb("qg", [P, HD]), sb("kg", [P, HD])
            hg, rg = sb("hg", [P, HD]), sb("rg", [P, HD])
            x = sb("x", [P, D])
            xh, xl = sb("xh", [P, D], F16), sb("xl", [P, D], F16)
            hTh, hTl = sb("hTh", [P, DC, P], F16), sb("hTl", [P, DC, P], F16)
            identh = sb("identh", [P, P], F16)
            bqf = sb("bqf", [P, 4, P])
            bi, gb = sb("bi", [P, 256]), sb("gb", [P, 256])
            cv, gc = sb("cv", [P, 256]), sb("gc", [P, 256])
            bqT, ef, fT = sb("bqT", [P, 2, P]), sb("ef", [P, 2, P]), sb("fT", [P, 2, P])
            kkT, bT = sb("kkT", [P, 2, P]), sb("bT", [P, 2, P])
            qe, qw = sb("qe", [P, 2, P]), sb("qw", [P, 2, P])
            kt = sb("kt", [P, 2, 4, P])
            k2T, k2, elast = sb("k2T", [P, 2, P]), sb("k2", [P, 2, P]), sb("elast", [P, 2])
            ones = sb("ones", [P, P])
            rt1, rt2 = sb("rt1", [P, 512]), sb("rt2", [P, 512])
            rpc, cks = sb("rpc", [P, 512]), sb("cks", [P, 256])
            cqkT, cqs = sb("cqkT", [P, 4, P]), sb("cqs", [P, 2, P])
            atth, attr = sb("atth", [P, 4, P]), sb("attr", [P, 4, P])
            qrp = sb("qrp", [P, 512])
            av, iw, ik2 = sb("av", [P, P]), sb("iw", [P, 8]), sb("ik2", [P, P])
            ak, sqk, ssk, rsk = sb("ak", [P, P]), sb("sqk", [P, P]), sb("ssk", [P, 2]), sb("rsk", [P, 2])
            ssa, rsa = sb("ssa", [P, 8]), sb("rsa", [P, 8])
            ga = sb("ga", [P, 512])
            sqo = sb("sqo", [P, 256])
            sso, rso = sb("sso", [P, 2, 4]), sb("rso", [P, 2, 4])
            yb, yc, ut = sb("yb", [P, 256]), sb("yc", [P, 256]), sb("ut", [P, 256])
            S2, R2 = sb("S2", [P, 2, P]), sb("R2", [P, 2, P])
            iqT, qT, kiT = sb("iqT", [P, 4, P]), sb("qT", [P, 4, P]), sb("kiT", [P, 2, P])
            ssx, rsx = sb("ssx", [P, 1]), sb("rsx", [P, 1])
            mhalf = sb("mhalf", [P, 8])
            lbl = sb("lbl", [P, 2, 2])
            sqa = sb("sqa", [P, 512])

            def ps(name):
                return ctx.enter_context(nc.psum_tensor(name, [P, 512], F32))

            PJ = [ps(f"PJ{i}") for i in range(PJ_BANKS)]
            TR = [ps("TR0"), ps("TR1")]
            ATT, OU = ps("ATT"), ps("OU")
            trv = [t[:].rearrange("p (c t) -> p c t", c=4) for t in TR]
            trh = [t[:].bitcast(F16).rearrange("p (c t) -> p c t", c=DC) for t in TR]
            attv = ATT[:].rearrange("p (c t) -> p c t", c=4)

            consts, states_in, x_in = sem("consts"), sem("states_in"), sem("x_in")
            w_stage_in = [sem(f"w_stage_in{i}") for i in range(W_STAGES)]
            w_hi_ok, w_lo_ok = sem("w_hi_ok"), sem("w_lo_ok")
            chunks = [(g, c) for g in range(NG) for c in range(DC)]
            prep = sem("prep")
            x_sq, x_ms, x_rs, xh_ok, xl_ok, xT_ok, hTh_ok, hTl_ok = (sem(n) for n in (
                "x_sq", "x_ms", "x_rs", "xh_ok", "xl_ok", "xT_ok", "hTh_ok", "hTl_ok"))
            proj, act_read, dve_read = sem("proj"), sem("act_read"), sem("dve_read")
            bqfT_ok, bq_copied, ef_ok, f_ok, lf_ok, b_ok, eb_ok, kt_ok, hq_ok = (sem(n) for n in (
                "bqfT_ok", "bq_copied", "ef_ok", "f_ok", "lf_ok", "b_ok", "eb_ok", "kt_ok", "hq_ok"))
            k2t_ok, k2_ok, atth_ok, atth_m = (sem(n) for n in ("k2t_ok", "k2_ok", "atth_ok", "atth_m"))
            rpc_ok, cqkT_ok, cqkT_c, cqs_ok, attr_ok, attr_m = (sem(n) for n in (
                "rpc_ok", "cqkT_ok", "cqkT_c", "cqs_ok", "attr_ok", "attr_m"))
            oh_ok, or_ok, sqo_ok, msoh, rsoh, sh_ok, yb_ok = (sem(n) for n in (
                "oh_ok", "or_ok", "sqo_ok", "msoh", "rsoh", "sh_ok", "yb_ok"))
            rpi_ok, iqT_ok, iqT_c = sem("rpi_ok"), sem("iqT_ok"), sem("iqT_c")
            sqk_ok, msk, rsk_ok, ki_ok, kiT_ok, kiT_c, av_ok = (sem(n) for n in (
                "sqk_ok", "msk", "rsk_ok", "ki_ok", "kiT_ok", "kiT_c", "av_ok"))
            sqa_ok, msa, rsa_ok, aq_ok, aqT_ok, aqT_c = (sem(n) for n in (
                "sqa_ok", "msa", "rsa_ok", "aq_ok", "aqT_ok", "aqT_c"))
            dve_step, even_heads = sem("dve_step"), sem("even_heads")
            st_q, st_iq, st_ki, st_k, st_v, st_y, st_st = (sem(n) for n in (
                "st_q", "st_iq", "st_ki", "st_k", "st_v", "st_y", "st_st"))

            def weights(g, c, half):
                n0, wd = DC * GOFF[GROUPS[g][0]] + c * GROUPS[g][1], GROUPS[g][1]
                return half[:, n0:n0 + wd]

            def head_square(state, j):
                r = slice(HD * (j % 2), HD * (j % 2) + HD)
                return state[r, j // 2, r]

            def wait(eng, s, value):
                if isinstance(value, int) and value <= 0:
                    return
                eng.wait_ge(s, value)

            block = ctx.enter_context(nc.Block())

            @block.sync
            def _(sp):
                def load_x(b):
                    r0, T = rows(b)
                    sp.dma_start(x[0:T, :], xs[l, r0:r0 + T, :]).then_inc(x_in, 16)

                load_x(0)
                for d, s in ((rope[:], c_rope[:, :, :]), (causal[:], c_causal[:, :]), (dmat[:], c_dmat[:, :, :]),
                             (lrow[:], c_lrow[:, :, :]), (ksc[:], c_ksc[:, :, :]), (gt[:], c_gt[:, :, :]),
                             (bmask[:], c_bmask[:, :]), (ng[:], norm_g[l, :, :]),
                             (qg[:], q_g[l, :, :]), (kg[:], k_g[l, :, :]), (hg[:], h_g[l, :, :]), (rg[:], r_g[l, :, :])):
                    sp.dma_start(d, s).then_inc(consts, 16)
                for i, (g, c) in enumerate(chunks):
                    if i >= W_STAGES:
                        sp.wait_ge(w_lo_ok, i - W_STAGES + 1)
                    sp.dma_start(wst[:, i % W_STAGES, 0:GROUPS[g][1]],
                                 weights(g, c, w_in[l])).then_inc(w_stage_in[i % W_STAGES], 16)
                for b in range(NBLK):
                    r0, T = rows(b)
                    dst_k, dst_v, dst_i = (k_p, v_p, ik_p) if b < NB else (k_s, v_s, ik_s)
                    o0 = r0 if b < NB else 0
                    if b == NB:
                        sp.wait_ge(sh_ok, 2 * NB)
                        for j in range(4):
                            sp.dma_start(hg_p[l, j, :, :], head_square(S2, j)).then_inc(st_st, 16)
                            sp.dma_start(rt_p[l, j, :, :], head_square(R2, j)).then_inc(st_st, 16)
                        sp.wait_ge(st_st, 8 * 16)
                        for j in range(4):
                            sp.dma_start(head_square(S2, j), st_h[l, j, :, :]).then_inc(states_in, 16)
                            sp.dma_start(head_square(R2, j), st_r[l, j, :, :]).then_inc(states_in, 16)
                    if b < NB:
                        sp.wait_ge(xl_ok, b + 1)
                        load_x(b + 1)
                    sp.wait_ge(yb_ok, 2 * b + 1)
                    sp.dma_start(y_d[b, 0:T, 512:768], yb[0:T, :]).then_inc(st_y, 16)
                    sp.wait_ge(av_ok, b + 1)
                    sp.dma_start(dst_v[l, o0:o0 + T, :], av[0:T, :]).then_inc(st_v, 16)
                    sp.dma_start(iw_d[b, 0:T, :], iw[0:T, :]).then_inc(st_v, 16)
                    sp.wait_ge(iqT_c, b + 1)
                    sp.dma_start(iqT_d[b, :, 0:4 * T], iqT[:, :, 0:T]).then_inc(st_iq, 16)
                    sp.wait_ge(ki_ok, b + 1)
                    sp.dma_start(dst_k[l, o0:o0 + T, :], ak[0:T, :]).then_inc(st_k, 16)
                    sp.dma_start(dst_i[l, o0:o0 + T, :], ik2[0:T, 0:HD]).then_inc(st_k, 16)
                    sp.wait_ge(kiT_c, b + 1)
                    sp.dma_start(kT_d[:, r0:r0 + T], kiT[:, 0, 0:T]).then_inc(st_ki, 16)
                    sp.dma_start(ikT_d[:, r0:r0 + T], kiT[:, 1, 0:T]).then_inc(st_ki, 16)
                    sp.wait_ge(yb_ok, 2 * b + 2)
                    sp.dma_start(y_d[b, 0:T, 768:1024], yc[0:T, :]).then_inc(st_y, 16)
                    sp.wait_ge(dve_read, len(DVE_G) * (b + 1))
                    sp.dma_start(y_d[b, 0:T, 0:512], ga[0:T, :]).then_inc(st_y, 16)
                    sp.wait_ge(aqT_c, b + 1)
                    sp.dma_start(qT_d[b, :, 0:4 * T], qT[:, :, 0:T]).then_inc(st_q, 16)
                sp.wait_ge(sh_ok, 2 * NBLK)
                for j in range(4):
                    sp.dma_start(hg_s[l, j, :, :], head_square(S2, j)).then_inc(st_st, 16)
                    sp.dma_start(rt_s[l, j, :, :], head_square(R2, j)).then_inc(st_st, 16)
                sp.wait_ge(st_st, 16 * 16)
                sp.wait_ge(st_q, 16 * NBLK)
                sp.wait_ge(st_iq, 16 * NBLK)
                sp.wait_ge(st_ki, 32 * NBLK)
                sp.wait_ge(st_k, 32 * NBLK)
                sp.wait_ge(st_v, 32 * NBLK)
                sp.wait_ge(st_y, 48 * NBLK)

            @block.tensor
            def _(pe):
                mm = nc.tensor.matmul

                def transposes(dst, src, T):
                    for c, s in enumerate(src):
                        last = nc.tensor.transpose(dst[:, c, 0:T], s, ident[0:T, 0:T])
                    return last

                def x_transposes(t):
                    pe.wait_ge(xl_ok, t + 1)
                    wait(pe, kiT_c, t)
                    wait(pe, iqT_c, t)
                    for bank, src in enumerate((xh, xl)):
                        for k in range(DC):
                            last = nc.tensor.transpose(trh[bank][:, k, :], src[:, k * P:(k + 1) * P], identh[:])
                        last.then_inc(xT_ok, 1)

                def project(t, T, n):
                    g = GI[n]
                    wd = GROUPS[g][1]
                    if not isinstance(t, int) or t > 0 or g >= PJ_BANKS:
                        pn = GROUPS[(g - PJ_BANKS) % NG][0]
                        tt = t if g >= PJ_BANKS else t - 1
                        if pn in ACT_G:
                            pe.wait_ge(act_read, tt * len(ACT_G) + ACT_G[pn])
                        if pn in DVE_G:
                            pe.wait_ge(dve_read, tt * len(DVE_G) + DVE_G[pn])
                    if isinstance(t, int) and t == 0:
                        pe.wait_ge(w_lo_ok, DC * (g + 1))
                    out = PJ[g % PJ_BANKS][0:T, 0:wd]
                    for c in range(DC):
                        mm(out, hTh[:, c, 0:T], weights(g, c, wh), start=(c == 0), stop=False)
                        mm(out, hTh[:, c, 0:T], weights(g, c, wl), start=False, stop=False)
                        last = mm(out, hTl[:, c, 0:T], weights(g, c, wh), start=False, stop=(c == DC - 1))
                    last.then_inc(proj, 1)

                def block_of(t, T):
                    pe.wait_ge(hTh_ok, t + 1)
                    pe.wait_ge(hTl_ok, t + 1)
                    project(t, T, "bqf")
                    project(t, T, "big")
                    pe.wait_ge(act_read, t * len(ACT_G) + ACT_G["bqf"])
                    transposes(trv[0], [bqf[0:T, c, :] for c in range(4)], T).then_inc(bqfT_ok, 1)
                    project(t, T, "cqk")
                    project(t, T, "cvg")
                    project(t, T, "iq")
                    pe.wait_ge(rpc_ok, t + 1)
                    transposes(trv[1], [rpc[0:T, c * P:(c + 1) * P] for c in range(4)], T).then_inc(cqkT_ok, 1)
                    pe.wait_ge(hq_ok, t + 1)
                    pe.wait_ge(bq_copied, t + 1)
                    pe.wait_ge(f_ok, t + 1)
                    for p in range(2):
                        last = nc.tensor.transpose(TR[0][0:T, p * P:(p + 1) * P], k2T[:, p, 0:T], ident[:])
                    last.then_inc(k2t_ok, 1)
                    wait(pe, aqT_c, t)
                    for h in (0, 2, 1, 3):
                        p, r = h // 2, slice(64 * (h % 2), 64 * (h % 2) + 64)
                        if h == 1:
                            last.then_inc(even_heads, 1)
                            pe.wait_ge(even_heads, 2 * t + 1)
                        for i in reversed(range(T // WIN)):
                            m = (WIN, 2 * WIN, P, P)[i]
                            q = qe if i == 0 else qw
                            last = mm(ATT[0:m, h * P + i * WIN:h * P + (i + 1) * WIN], kt[r, p, i, 0:m],
                                      q[r, p, i * WIN:(i + 1) * WIN], start=True, stop=True)
                    last.then_inc(atth_ok, 1)
                    project(t, T, "kvi")
                    pe.wait_ge(atth_m, t + 1)
                    pe.wait_ge(k2_ok, t + 1)
                    wait(pe, sh_ok, 2 * t)
                    wait(pe, yb_ok, 2 * t)
                    if isinstance(t, int) and t == NB:
                        pe.wait_ge(states_in, 8 * 16)
                    recurrence(T, qe, S2, atth, bi, k2, oh_ok)
                    pe.wait_ge(cqkT_c, t + 1)
                    pe.wait_ge(cqs_ok, t + 1)
                    for h in (0, 2, 1, 3):
                        p, r = h // 2, slice(64 * (h % 2), 64 * (h % 2) + 64)
                        if h == 1:
                            last.then_inc(even_heads, 1)
                            pe.wait_ge(even_heads, 2 * t + 2)
                        last = mm(ATT[0:T, h * P:h * P + T], cqkT[r, 2 + p, 0:T], cqkT[r, p, 0:T], start=True, stop=True)
                    last.then_inc(attr_ok, 1)
                    project(t, T, "aq")
                    pe.wait_ge(rpi_ok, t + 1)
                    transposes(trv[1], [qrp[0:T, c * P:(c + 1) * P] for c in range(4)], T).then_inc(iqT_ok, 1)
                    pe.wait_ge(attr_m, t + 1)
                    pe.wait_ge(sh_ok, 2 * t + 1)
                    pe.wait_ge(yb_ok, 2 * t + 1)
                    recurrence(T, cqs, R2, attr, cv, cks, or_ok)
                    pe.wait_ge(ki_ok, t + 1)
                    for c, s in enumerate((ak, ik2)):
                        last = nc.tensor.transpose(trv[0][:, c, 0:T], s[0:T, :], ident[0:T, 0:T])
                    last.then_inc(kiT_ok, 1)
                    if T == P:
                        x_transposes(t + 1)
                    project(t, T, "ag")
                    pe.wait_ge(aq_ok, t + 1)
                    transposes(attv, [qrp[0:T, c * P:(c + 1) * P] for c in range(4)], T).then_inc(aqT_ok, 1)

                def recurrence(T, q, state, att, v, kend, done):
                    for p in range(2):
                        mm(OU[0:T, p * P:(p + 1) * P], q[:, p, 0:T], state[:, p, :], start=(p == 0), stop=False)
                    for h in range(4):
                        mm(OU[0:T, h * HD:(h + 1) * HD], att[0:T, h, 0:T], v[0:T, h * HD:(h + 1) * HD],
                           start=False, stop=(h == 3))
                    for p in range(2):
                        ke = kend[0:T, p, :] if len(kend.shape) == 3 else kend[0:T, p * P:(p + 1) * P]
                        last = mm(OU[:, 256 + p * P:256 + (p + 1) * P], ke, v[0:T, p * P:(p + 1) * P], start=True, stop=True)
                    last.then_inc(done, 1)

                pe.wait_ge(prep, 1)
                x_transposes(0)
                block_of(0, P)
                if NB > 1:
                    with pe.Fori(1, NB) as t:
                        block_of(t, P)
                block_of(NB, TS)

            @block.scalar
            def _(act):
                A = nc.scalar.activation

                def split_weights(g0, g1):
                    for i in range(DC * g0, DC * g1):
                        g, c = chunks[i]
                        act.wait_ge(w_stage_in[i % W_STAGES], 16 * (i // W_STAGES + 1))
                        A(weights(g, c, wh), wst[:, i % W_STAGES, 0:GROUPS[g][1]], ACT.Copy,
                          scale=ng[:, c:c + 1]).then_inc(w_hi_ok, 1)

                def x_squares(t):
                    act.wait_ge(x_in, 16 * t + 16)
                    A(xh[:].bitcast(BF16), x[:], ACT.Square, accum_out=ssx[:]).then_inc(x_sq, 1)

                def x_high(t):
                    act.wait_ge(x_rs, t + 1)
                    A(xh[:], x[:], ACT.Copy, scale=rsx[:, 0:1]).then_inc(xh_ok, 1)

                def hT_high(t):
                    act.wait_ge(xT_ok, 2 * t + 1)
                    A(hTh[:], trh[0], ACT.Copy).then_inc(hTh_ok, 1)

                def read_proj(t, n):
                    act.wait_ge(proj, t * NG + GI[n] + 1)

                def block_of(t, T):
                    pj = {n: PJ[GI[n] % PJ_BANKS] for n in GI}
                    read_proj(t, "bqf")
                    wait(act, bqfT_ok, t)
                    A(bqf[0:T, :, :], pj["bqf"][0:T, :].rearrange("p (c n) -> p c n", c=4), ACT.Copy, scale=UNSCALE).then_inc(act_read, 1)
                    read_proj(t, "big")
                    wait(act, oh_ok, t)
                    A(bi[0:T, :], pj["big"][0:T, 0:256], ACT.Copy, scale=UNSCALE)
                    wait(act, yb_ok, 2 * t)
                    A(gb[0:T, :], pj["big"][0:T, 256:512], ACT.Tanh, scale=UNSCALE / 2).then_inc(act_read, 1)
                    act.wait_ge(bqfT_ok, t + 1)
                    A(ef[:, :, 0:T], trv[0][:, 2:4, 0:T], ACT.Exp, scale=-1.0).then_inc(ef_ok, 1)
                    A(bqT[:, :, 0:T], trv[0][:, 0:2, 0:T], ACT.Copy).then_inc(bq_copied, 1)
                    if isinstance(t, int) and t == 0:
                        split_weights(3, 5)
                    act.wait_ge(f_ok, t + 1)
                    A(fT[:, :, 0:T], fT[:, :, 0:T], ACT.Ln).then_inc(lf_ok, 1)
                    act.wait_ge(b_ok, t + 1)
                    wait(act, kt_ok, t)
                    wait(act, atth_ok, t)
                    A(qe[:, :, 0:T], bT[:, :, 0:T], ACT.Exp).then_inc(eb_ok, 1)
                    if T > WIN:
                        A(qw[:, :, WIN:T], qw[:, :, WIN:T], ACT.Exp).then_inc(eb_ok, 1)
                    else:
                        A(qw[:, :, 0:T], bT[:, :, 0:T], ACT.Exp).then_inc(eb_ok, 1)
                    for p in range(2):
                        A(k2T[:, p, 0:T], bT[:, p, 0:T], ACT.Exp, scale=-1.0, bias=bT[:, p, T - 1:T])
                        for i in range(T // WIN):
                            ref = 0.0 if i == 0 else bT[:, p, i * WIN - 1:i * WIN]
                            A(kt[:, p, i, 0:(i + 1) * WIN], bT[:, p, 0:(i + 1) * WIN], ACT.Exp, scale=-1.0, bias=ref)
                    A(elast[:], bT[:, :, T - 1], ACT.Exp).then_inc(kt_ok, 1)
                    if isinstance(t, int) and t == 0:
                        split_weights(5, 7)
                    read_proj(t, "cvg")
                    wait(act, or_ok, t)
                    A(cv[0:T, :], pj["cvg"][0:T, 0:256], ACT.Copy, scale=UNSCALE)
                    wait(act, yb_ok, 2 * t)
                    A(gc[0:T, :], pj["cvg"][0:T, 256:512], ACT.Tanh, scale=UNSCALE / 2).then_inc(act_read, 1)
                    act.wait_ge(cqkT_ok, t + 1)
                    wait(act, attr_ok, t)
                    A(cqkT[:, :, 0:T], trv[1][:, :, 0:T], ACT.Copy).then_inc(cqkT_c, 1)
                    act.wait_ge(k2t_ok, t + 1)
                    A(k2[0:T, :, :], TR[0][0:T, 0:256].rearrange("p (c n) -> p c n", c=2), ACT.Copy).then_inc(k2_ok, 1)
                    if isinstance(t, int) and t == 0:
                        split_weights(7, 8)
                    if T == P:
                        x_squares(t + 1)
                    act.wait_ge(oh_ok, t + 1)
                    wait(act, msoh, 2 * t)
                    A(sqo[0:T, :], OU[0:T, 0:256], ACT.Square).then_inc(sqo_ok, 1)
                    read_proj(t, "kvi")
                    kvi = pj["kvi"]
                    wait(act, st_v, 32 * t)
                    A(av[0:T, :], kvi[0:T, 128:256], ACT.Copy, scale=UNSCALE)
                    A(iw[0:T, :], kvi[0:T, 320:328], ACT.Copy, scale=IDX_W_SCALE * UNSCALE).then_inc(av_ok, 1)
                    wait(act, msk, t)
                    A(sqk[0:T, :], kvi[0:T, 0:128], ACT.Square, scale=UNSCALE).then_inc(sqk_ok, 1)
                    if T == P:
                        x_high(t + 1)
                    read_proj(t, "aq")
                    wait(act, aq_ok, t)
                    A(sqa[0:T, :], pj["aq"][0:T, :], ACT.Square, scale=UNSCALE).then_inc(act_read, 1)
                    act.wait_ge(iqT_ok, t + 1)
                    wait(act, st_iq, 16 * t)
                    A(iqT[:, :, 0:T], trv[1][:, :, 0:T], ACT.Copy).then_inc(iqT_c, 1)
                    act.wait_ge(or_ok, t + 1)
                    act.wait_ge(msoh, 2 * t + 1)
                    A(sqo[0:T, :], OU[0:T, 0:256], ACT.Square).then_inc(sqo_ok, 1)
                    act.wait_ge(kiT_ok, t + 1)
                    wait(act, st_ki, 32 * t)
                    A(kiT[:, :, 0:T], trv[0][:, 0:2, 0:T], ACT.Copy).then_inc(kiT_c, 1)
                    read_proj(t, "ag")
                    if T == P:
                        hT_high(t + 1)
                    wait(act, st_y, 48 * t)
                    A(ga[0:T, :], pj["ag"][0:T, :], ACT.Tanh, scale=UNSCALE / 2).then_inc(act_read, 1)
                    act.wait_ge(aqT_ok, t + 1)
                    wait(act, st_q, 16 * t)
                    A(qT[:, :, 0:T], attv[:, :, 0:T], ACT.Copy).then_inc(aqT_c, 1)

                act.wait_ge(prep, 1)
                x_squares(0)
                x_high(0)
                split_weights(0, 1)
                hT_high(0)
                split_weights(1, 3)
                block_of(0, P)
                if NB > 1:
                    with act.Fori(1, NB) as t:
                        block_of(t, P)
                block_of(NB, TS)

            @block.gpsimd
            def _(pool):
                def rsqrt(src_ok, done, out, in_, value):
                    pool.wait_ge(src_ok, value)
                    nc.gpsimd.tensor_tensor(out, in_, mhalf[0:in_.shape[0], 0:in_.shape[1]], ALU.pow).then_inc(done, 1)

                def block_of(t, T):
                    if T == P:
                        rsqrt(x_ms, x_rs, rsx[:], ssx[:], t + 2)
                    rsqrt(msoh, rsoh, rso[0:T, 0, :], sso[0:T, 0, :], 2 * t + 1)
                    rsqrt(msk, rsk_ok, rsk[0:T, :], ssk[0:T, :], t + 1)
                    rsqrt(msa, rsa_ok, rsa[0:T, :], ssa[0:T, :], t + 1)
                    rsqrt(msoh, rsoh, rso[0:T, 1, :], sso[0:T, 1, :], 2 * t + 2)

                pool.wait_ge(prep, 1)
                rsqrt(x_ms, x_rs, rsx[:], ssx[:], 1)
                block_of(0, P)
                if NB > 1:
                    with pool.Fori(1, NB) as t:
                        block_of(t, P)
                block_of(NB, TS)

            @block.vector
            def _(dve):
                V = nc.vector

                def bc(ap, shape, axis):
                    return ap.unsqueeze(axis).broadcast_to(shape)

                def mean_square(step, ss, sq, n, done, width=HD):
                    step(V.tensor_reduce(ss, sq.rearrange("p (h d) -> p h d", h=n), AX_X, ALU.add))
                    V.tensor_scalar(ss, ss, 1.0 / width, EPS, ALU.mult, ALU.add).then_inc(done, 1)

                def rotate(step, t, T, src, dst, nh, read=(), done=()):
                    cos, sin = rope[0:T, t, 0:HALF], rope[0:T, t, HALF:HD]
                    s3 = src.rearrange("p (g d) -> p g d", d=HALF)
                    s4 = src.rearrange("p (h g d) -> p h g d", g=2, d=HALF)
                    d4 = dst.rearrange("p (h g d) -> p h g d", g=2, d=HALF)
                    a, b = rt1[0:T, 0:nh * HD], rt2[0:T, 0:nh * HD]
                    a3 = a.rearrange("p (g d) -> p g d", d=HALF)
                    a4 = a.rearrange("p (h g d) -> p h g d", g=2, d=HALF)
                    b4 = b.rearrange("p (h g d) -> p h g d", g=2, d=HALF)
                    step(V.tensor_tensor(a3, s3, bc(cos, [T, 2 * nh, HALF], 1), ALU.mult))
                    step(V.tensor_tensor(b4[:, :, 0, :], s4[:, :, 1, :], bc(sin, [T, nh, HALF], 1), ALU.mult))
                    step(V.tensor_tensor(b4[:, :, 1, :], s4[:, :, 0, :], bc(sin, [T, nh, HALF], 1), ALU.mult), *read)
                    step(V.tensor_tensor(d4[:, :, 0, :], a4[:, :, 0, :], b4[:, :, 0, :], ALU.subtract))
                    step(V.tensor_tensor(d4[:, :, 1, :], a4[:, :, 1, :], b4[:, :, 1, :], ALU.add), *done)

                def state_update(step, state, decay, done, value):
                    u = OU[:, 256:512].rearrange("p (c n) -> p c n", c=2)
                    ut3 = ut[:].rearrange("p (c n) -> p c n", c=2)
                    step(V.tensor_tensor(ut3, u, bc(bmask[:], [P, 2, P], 1), ALU.mult))
                    for p in range(2):
                        step(V.scalar_tensor_tensor(out=state[:, p, :], in0=state[:, p, :], scalar=decay[:, p:p + 1],
                                                    in1=ut3[:, p, :], op0=ALU.mult, op1=ALU.add),
                             *((done, value) if p == 1 else ()))

                def block_of(t, T):
                    base = t * DVE_STEPS if isinstance(t, int) else dve.snap(t * DVE_STEPS)
                    n = [0]

                    def step(ins, done=None, value=None):
                        if done is not None:
                            ins.then_inc(done, 1)
                            dve.wait_ge(done, value)
                            return
                        n[0] += 1
                        ins.then_inc(dve_step, 1)
                        dve.wait_ge(dve_step, base + n[0])

                    def was_read(group):
                        return dve_read, t * len(DVE_G) + DVE_G[group]

                    kind = 0 if T == P else 1
                    nw = T // WIN
                    pj = {g: PJ[GI[g] % PJ_BANKS] for g in GI}

                    def read_proj(g):
                        dve.wait_ge(proj, t * NG + GI[g] + 1)

                    def gate(out, x, group):
                        step(V.scalar_tensor_tensor(out=out, in0=out, scalar=1.0, in1=x, op0=ALU.add, op1=ALU.mult),
                             *was_read(group))

                    first = isinstance(t, int) and t == 0
                    if first:
                        split_weights(3, 5)
                    dve.wait_ge(ef_ok, t + 1)
                    fv = fT[:, :, 0:T]
                    step(V.tensor_scalar(ef[:, :, 0:T], ef[:, :, 0:T], 1.0, None, ALU.add))
                    step(V.reciprocal(ef[:, :, 0:T], ef[:, :, 0:T]))
                    for p in range(2):
                        step(V.tensor_scalar(fT[:, p, 0:T], ef[:, p, 0:T], lbl[:, 1, p:p + 1], lbl[:, 0, p:p + 1],
                                             ALU.mult, ALU.add))
                    dve.wait_ge(bq_copied, t + 1)
                    step(V.tensor_scalar(kkT[:, :, 0:T], fv, -1.0, 1.0, ALU.mult, ALU.add), f_ok, t + 1)
                    dve.wait_ge(act_read, t * len(ACT_G) + ACT_G["big"])
                    gate(gb[0:T, :], pj["big"][0:T, 256:512], "big")
                    h3 = [T, 4, HD]
                    gb3, gc3 = (g[0:T, :].rearrange("p (h d) -> p h d", h=4) for g in (gb, gc))
                    step(V.tensor_tensor(gb3, gb3, bc(hg[0:T, :], h3, 1), ALU.mult))
                    dve.wait_ge(lf_ok, t + 1)
                    for p in range(2):
                        step(V.tensor_tensor_scan(bT[:, p, 0:T], ones[:, 0:T], fT[:, p, 0:T], 0.0, ALU.mult, ALU.add),
                             *((b_ok, t + 1) if nw == 1 and p == 1 else ()))
                    for p in range(2):
                        if nw > 1:
                            if p == 0:
                                wait(dve, atth_ok, t)
                            step(V.tensor_tensor(qw[:, p, WIN:T].rearrange("p (w s) -> p w s", s=WIN),
                                                 bT[:, p, WIN:T].rearrange("p (w s) -> p w s", s=WIN),
                                                 bT[:, p, WIN - 1:T - 1:WIN].unsqueeze(2).broadcast_to([P, nw - 1, WIN]),
                                                 ALU.subtract), *((b_ok, t + 1) if p == 1 else ()))
                    dve.wait_ge(eb_ok, 2 * t + 2)
                    step(V.tensor_tensor(qe[:, :, 0:T], qe[:, :, 0:T], bqT[:, :, 0:T], ALU.mult))
                    if nw > 1:
                        step(V.tensor_tensor(qw[:, :, WIN:T], qw[:, :, WIN:T], bqT[:, :, WIN:T], ALU.mult))
                    dve.wait_ge(kt_ok, t + 1)
                    for p in range(2):
                        step(V.tensor_tensor(kt[:, p, 0:nw, 0:T], kt[:, p, 0:nw, 0:T],
                                             bc(kkT[:, p, 0:T], [P, nw, T], 1), ALU.mult))
                    step(V.tensor_tensor(k2T[:, :, 0:T], k2T[:, :, 0:T], kkT[:, :, 0:T], ALU.mult), hq_ok, t + 1)
                    if first:
                        split_weights(5, 7)
                    read_proj("cqk")
                    wait(dve, cqkT_ok, t)
                    wait(dve, or_ok, t)
                    rotate(step, t, T, pj["cqk"][0:T, :], rpc[0:T, :], 8, was_read("cqk"))
                    step(V.tensor_tensor(cks[0:T, :].rearrange("p (h d) -> p h d", h=4),
                                         rpc[0:T, 256:512].rearrange("p (h d) -> p h d", h=4),
                                         ksc[0:T, kind, :].unsqueeze(2).broadcast_to(h3), ALU.mult), rpc_ok, t + 1)
                    dve.wait_ge(act_read, t * len(ACT_G) + ACT_G["cvg"])
                    gate(gc[0:T, :], pj["cvg"][0:T, 256:512], "cvg")
                    step(V.tensor_tensor(gc3, gc3, bc(rg[0:T, :], h3, 1), ALU.mult))
                    dve.wait_ge(cqkT_c, t + 1)
                    step(V.tensor_tensor(cqs[:, :, 0:T], trv[1][:, 0:2, 0:T], lrow[:, :, 0:T], ALU.mult), cqs_ok, t + 1)
                    dve.wait_ge(atth_ok, t + 1)
                    attp = ATT[:].rearrange("p (h t) -> p h t", h=4)
                    for i in range(nw):
                        m = (i + 1) * WIN
                        tw = slice(i * WIN, m)
                        step(V.tensor_tensor(atth[0:m, :, tw], attp[0:m, :, tw], bc(causal[0:m, tw], [m, 4, WIN], 1), ALU.mult),
                             *((atth_m, t + 1) if i == nw - 1 else ()))
                    if first:
                        split_weights(7, 8)
                    if T == P:
                        x_mean_square(t + 1)
                    read_proj("iq")
                    wait(dve, aqT_ok, t)
                    rotate(step, t, T, pj["iq"][0:T, :], qrp[0:T, :], 8, was_read("iq"), (rpi_ok, t + 1))

                    def mixer_out(j, state, decay, y, gate):
                        dve.wait_ge(sqo_ok, 2 * t + 1 + j)
                        mean_square(step, sso[0:T, j, :], sqo[0:T, :], 4, msoh)
                        state_update(step, state, decay, sh_ok, 2 * t + 1 + j)
                        dve.wait_ge(rsoh, 2 * t + 1 + j)
                        wait(dve, st_y, 48 * t)
                        y3 = y[0:T, :].rearrange("p (h d) -> p h d", h=4)
                        o3 = OU[0:T, 0:256].rearrange("p (h d) -> p h d", h=4)
                        step(V.tensor_tensor(y3, o3, rso[0:T, j, :].unsqueeze(2).broadcast_to(h3), ALU.mult))
                        step(V.tensor_tensor(y[0:T, :], y[0:T, :], gate[0:T, :], ALU.mult), yb_ok, 2 * t + 1 + j)

                    mixer_out(0, S2, elast, yb, gb)
                    dve.wait_ge(attr_ok, t + 1)
                    step(V.tensor_tensor(attr[0:T, :, 0:T], attp[0:T, :, 0:T], dmat[0:T, :, 0:T], ALU.mult), attr_m, t + 1)
                    kvi = pj["kvi"]
                    read_proj("kvi")
                    dve.wait_ge(sqk_ok, t + 1)
                    mean_square(step, ssk[0:T, :], sqk[0:T, :], 2, msk)
                    wait(dve, kiT_ok, t)
                    wait(dve, st_k, 32 * t)
                    rotate(step, t, T, kvi[0:T, 256:320], ik2[0:T, 0:HD], 1)
                    step(V.tensor_copy(ik2[0:T, HD:P], ik2[0:T, 0:HD]))
                    dve.wait_ge(rsk_ok, t + 1)
                    k3 = sqk[0:T, :].rearrange("p (h d) -> p h d", h=2)
                    step(V.tensor_tensor(k3, kvi[0:T, 0:P].rearrange("p (h d) -> p h d", h=2),
                                         rsk[0:T, :].unsqueeze(2).broadcast_to([T, 2, HD]), ALU.mult), *was_read("kvi"))
                    step(V.tensor_tensor(k3, k3, bc(kg[0:T, :], [T, 2, HD], 1), ALU.mult))
                    rotate(step, t, T, sqk[0:T, :], ak[0:T, :], 2, (), (ki_ok, t + 1))
                    if T == P:
                        x_low(t + 1)
                    dve.wait_ge(act_read, t * len(ACT_G) + ACT_G["aq"])
                    mean_square(step, ssa[0:T, :], sqa[0:T, :], 8, msa)
                    dve.wait_ge(rsa_ok, t + 1)
                    a3 = sqa[0:T, :].rearrange("p (h d) -> p h d", h=8)
                    step(V.tensor_tensor(a3, pj["aq"][0:T, :].rearrange("p (h d) -> p h d", h=8),
                                         rsa[0:T, :].unsqueeze(2).broadcast_to([T, 8, HD]), ALU.mult), *was_read("aq"))
                    step(V.tensor_tensor(a3, a3, bc(qg[0:T, :], [T, 8, HD], 1), ALU.mult))
                    dve.wait_ge(iqT_ok, t + 1)
                    rotate(step, t, T, sqa[0:T, :], qrp[0:T, :], 8, (), (aq_ok, t + 1))
                    if T == P:
                        read_proj("ag")
                        hT_low(t + 1)
                    dve.wait_ge(or_ok, t + 1)
                    mixer_out(1, R2, gt[:, kind, :], yc, gc)
                    dve.wait_ge(act_read, t * len(ACT_G) + ACT_G["ag"])
                    gate(ga[0:T, :], pj["ag"][0:T, :], "ag")
                    if T == P:
                        assert n[0] == DVE_STEPS, n[0]

                def x_mean_square(t):
                    dve.wait_ge(x_sq, t + 1)
                    V.tensor_scalar(ssx[:], ssx[:], 1.0 / D, EPS, ALU.mult, ALU.add).then_inc(x_ms, 1)

                def x_low(t):
                    dve.wait_ge(xh_ok, t + 1)
                    V.scalar_tensor_tensor(out=xl[:], in0=x[:], scalar=rsx[:, 0:1], in1=xh[:], op0=ALU.mult,
                                           op1=ALU.subtract).then_inc(xl_ok, 1)

                def hT_low(t):
                    dve.wait_ge(xT_ok, 2 * t + 2)
                    V.tensor_copy(hTl[:], trh[1]).then_inc(hTl_ok, 1)

                def split_weights(g0, g1):
                    for i in range(DC * g0, DC * g1):
                        g, c = chunks[i]
                        dve.wait_ge(w_hi_ok, i + 1)
                        V.scalar_tensor_tensor(out=weights(g, c, wl), in0=wst[:, i % W_STAGES, 0:GROUPS[g][1]],
                                               scalar=ng[:, c:c + 1], in1=weights(g, c, wh), op0=ALU.mult,
                                               op1=ALU.subtract).then_inc(w_lo_ok, 1)

                V.memset(mhalf[:], -0.5)
                V.memset(ones[:], 1.0)
                V.memset(kt[:], 0.0)
                V.memset(atth[:], 0.0)
                V.memset(S2[:], 0.0)
                dve.wait_ge(consts, 16 * 12)
                V.tensor_scalar(ng[:], ng[:], W_SCALE, None, ALU.mult)
                V.tensor_scalar(rope[:], rope[:], UNSCALE, None, ALU.mult)
                V.tensor_scalar(hg[:], hg[:], UNSCALE / 2, None, ALU.mult)
                V.tensor_scalar(rg[:], rg[:], UNSCALE / 2, None, ALU.mult)
                V.tensor_copy(identh[:], ident[:])
                V.tensor_copy(lbl[:, 0, :], lbt[:, l, :])
                V.tensor_copy(lbl[:, 1, :], oml[:, l, :])
                V.memset(R2[:], 0.0).then_inc(prep, 1)
                dve.wait_ge(prep, 1)
                x_mean_square(0)
                x_low(0)
                split_weights(0, 1)
                hT_low(0)
                split_weights(1, 3)
                block_of(0, P)
                if NB > 1:
                    with dve.Fori(1, NB) as t:
                        block_of(t, P)
                block_of(NB, TS)

    def attention_half(l, sem):
        with ExitStack() as ctx:
            def sb(name, shape, dt=F32):
                return ctx.enter_context(nc.sbuf_tensor(name, shape, dt))

            wo = [sb("w_out_hi", [P, DC, D], F16), sb("w_out_lo", [P, DC, D], F16)]
            LS = PAST + TS
            keys = [[[sb(f"key{n}{h}_{c}", [P, L], F16) for h in ("h", "l")] for n in range(3)]
                    for c, L in (("p", SEQ), ("s", LS))]
            va = [sb("va_p", [P, NB, 2, HD + 1]), sb("va_s", [P, NPB + 1, 2, HD + 1])]
            stg = [sb("stg0", [P, max(2 * D, SEQ, LS)]), sb("stg1", [P, max(2 * D, SEQ, LS)])]
            identb = sb("identb", [P, 4, P], BF16)
            onesb = sb("onesb", [P, P], BF16)
            pw = sb("pw", [P, NIT + 1])
            WMAX = max(SEQ, LS)
            sc = [sb("sc0", [P, WMAX]), sb("sc1", [P, WMAX])]
            rl = sb("rl", [P, 4, 512])
            mneg = [sb("mneg0", [P, WMAX], BF16), sb("mneg1", [P, WMAX], BF16)]
            ghi = sb("ghi", [P, WMAX], BF16)
            junk = sb("junkb", [P, 2, 512], BF16)
            iqs, qs = sb("iqs", [P, 8 * P]), sb("qs", [P, 8 * P])
            iq16, q16 = sb("iq16", [P, 2, 8 * P], F16), sb("q16", [P, 2, 8 * P], F16)
            iw = sb("iwb", [P, 2, 8])
            yt, xr = sb("yt", [P, 2, D]), sb("xr", [P, 2, D])
            pt = sb("pt", [P, 4, 512])
            oT = sb("oT", [P, 2, 512])
            yTh, yTl = sb("yTh", [P, DC, P], F16), sb("yTl", [P, DC, P], F16)
            on, rs = sb("on", [P, 512]), sb("rs", [P, 8])
            mxt, mx = sb("mxt", [P, 8, 5]), sb("mx", [P, 8])
            md = sb("md", [P, 8, P], BF16)
            small = {n: sb(n, [P, 1]) for n in "rng mid cnt cnta cnt2 dlt lo hi chi need".split()}
            stp = sb("stp", [P, NIT + 1])

            SC = [ctx.enter_context(nc.psum_tensor(f"SC{i}", [P, 512], F32)) for i in range(4)]
            PV = [ctx.enter_context(nc.psum_tensor(f"PV{i}", [P, 512], F32)) for i in range(2)]
            X = [ctx.enter_context(nc.psum_tensor(f"X{i}", [P, 512], F32)) for i in range(2)]

            names = ("stg_in0 stg_in1 hi_ok lo_ok pair_ok b_vp b_vs b_const b_prep b_iq b_iw0 b_iw1 b_q b_y0 b_y1 b_x0 b_x1 b_st0 b_st1 "
                     "idx_ok relu_ok acc_ok qk_ok max_ok qkt_ok exp_ok pv_ok oT_ok oX_ok on_ok yX_ok yTh_ok yTl_ok op_ok "
                     "res_ok md_ok mx_ok mneg_ok q16_ok iq16_ok pair_hi mid_ok cnt_ok b_step")
            s = {n: sem(n) for n in names.split()}

            def keys_of(b):
                return (0, (b + 1) * P, K_P) if b < NB else (1, PAST + TS, K_S)

            def searched(b):
                _, W, K = keys_of(b)
                return W > K

            def tiles(W):
                return [(c, min(512, W - c)) for c in range(0, W, 512)]

            def key_blocks(W):
                return [(c, min(P, W - c)) for c in range(0, W, P)]

            def idx_load(b):
                return sum(searched(i) for i in range(b % 2, b + 1, 2))

            def idx_nth(b):
                return sum(searched(i) for i in range(b + 1))

            def idx_order(W):
                ts = tiles(W)
                for g in range(0, len(ts), 2):
                    for h in range(8):
                        for c0, wd in ts[g:g + 2]:
                            yield h, c0, wd, len(ts[g:g + 2])

            def act_share(W):
                return int(W * ACT_COUNTS) // 32 * 32

            def order(b):
                p0 = 0.0 if b == 0 else 13.0
                at = [(p0 + 1.7 * (i + 1) * rows(b)[1] / P, "key", i) for i in range(n_main(b))]
                if b + 1 < NBLK and searched(b + 1):
                    W = keys_of(b + 1)[1]
                    at += [(2.0 + W / 960 + i * (0.8 + (W - act_share(W)) / 960), "bisect", i) for i in range(NIT)]
                return [e[1:] for e in sorted(at)]

            items = [("p", n) for n in range(3)] + [("w", n) for n in range(DC // 2)] + [("s", n) for n in range(3)]
            W_ITEM, S_ITEM = 3, 3 + DC // 2

            def pair_of(i):
                kind, n = items[i]
                if kind == "w":
                    return (stg[i % 2][:, 0:2 * D].rearrange("p (c n) -> p c n", c=2), wo[0][:, 2 * n:2 * n + 2, :],
                            wo[1][:, 2 * n:2 * n + 2, :], W_SCALE)
                c = "ps".index(kind)
                return stg[i % 2][:, 0:(SEQ, LS)[c]], keys[c][n][0][:], keys[c][n][1][:], 1.0

            N_DMA = {("p", 0): 2, ("p", 1): 2, ("p", 2): 1, ("s", 0): 4, ("s", 1): 4, ("s", 2): 3}

            def staged(i):
                return s[f"stg_in{i % 2}"], 16 * sum(N_DMA.get(items[j], 1) for j in range(i % 2, i + 1, 2))

            def paired(i):
                return (s["lo_ok"], i + 1) if i < S_ITEM else (s["pair_ok"], i - S_ITEM + 1)

            def before(b, f):
                return sum(f(i) for i in range(b))

            def n_idx(b):
                return 8 * len(tiles(keys_of(b)[1])) if searched(b) else 0

            def n_qk(b):
                return 8 * len(tiles(keys_of(b)[1]))

            def n_main(b):
                return 2 * len(key_blocks(keys_of(b)[1]))

            block = ctx.enter_context(nc.Block())

            @block.sync
            def _(sp):
                def go(d, src, name):
                    sp.dma_start(d, src).then_inc(s[name], 16)

                def twice(dst, src, name):
                    go(dst[0:HD], src, name)
                    go(dst[HD:P], src, name)

                def load_idx(b):
                    r0, T = rows(b)
                    if not searched(b):
                        return
                    if idx_nth(b) > 1:
                        sp.wait_ge(s["iq16_ok"], 2 * idx_nth(b) - 2)
                    for kv in range(2):
                        twice(iqs[:, kv * 4 * T:(kv + 1) * 4 * T], iqT_d[b, kv * HD:(kv + 1) * HD, 0:4 * T], "b_iq")
                    if b >= 2 and searched(b - 2):
                        sp.wait_ge(s["acc_ok"], before(b - 1, n_idx))
                    go(iw[0:T, b % 2, :], iw_d[b, 0:T, :], f"b_iw{b % 2}")

                def load_q(b):
                    T = rows(b)[1]
                    if b >= 1:
                        sp.wait_ge(s["q16_ok"], 2 * b)
                    for kv in range(2):
                        twice(qs[:, kv * 4 * T:(kv + 1) * 4 * T], qT_d[b, kv * HD:(kv + 1) * HD, 0:4 * T], "b_q")

                def load_yx(b):
                    r0, T = rows(b)
                    if b >= 2:
                        sp.wait_ge(s["yX_ok"], b - 1)
                    go(yt[0:T, b % 2, :], y_d[b, 0:T, :], f"b_y{b % 2}")
                    if b >= 2:
                        sp.wait_ge(s[f"b_st{b % 2}"], 16 * (b // 2))
                    go(xr[0:T, b % 2, :], xs[l, r0:r0 + T, :], f"b_x{b % 2}")

                def load_item(i):
                    kind, n = items[i]
                    name, buf = f"stg_in{i % 2}", stg[i % 2]
                    if i >= 2:
                        sp.wait_ge(*paired(i - 2))
                    if kind == "w":
                        go(buf[:, 0:2 * D], w_out[l, :, 2 * n:2 * n + 2, :], name)
                        return
                    dst = buf[:, 0:SEQ] if kind == "p" else buf[:, PAST:LS]
                    cols = slice(0, SEQ) if kind == "p" else slice(SEQ, SEQ + TS)
                    if n == 2:
                        go(dst, ikT_d[:, cols], name)
                    else:
                        twice(dst, kT_d[n * HD:(n + 1) * HD, cols], name)
                    if kind == "s":
                        twice(buf[:, 0:PAST], cache_i[l, :, :] if n == 2 else cache_k[l, n * HD:(n + 1) * HD, :], name)

                load_q(0)
                load_item(0)
                load_item(1)
                load_idx(0)
                load_yx(0)
                for h in range(2):
                    go(va[0][:, :, h, 0:HD], v_p[l, :, h * HD:(h + 1) * HD].rearrange("(b p) d -> p b d", p=P), "b_vp")
                go(pw[:], c_pow[:, :], "b_const")
                load_item(2)
                load_q(1)
                load_item(3)
                load_idx(1)
                load_yx(1)
                load_item(4)
                for h in range(2):
                    go(va[1][:, 0:NPB, h, 0:HD], cache_v[l, :, :, h * HD:(h + 1) * HD], "b_vs")
                    go(va[1][0:TS, NPB, h, 0:HD], v_s[l, :, h * HD:(h + 1) * HD], "b_vs")
                for b in range(NBLK):
                    r0, T = rows(b)
                    if b + 2 < NBLK:
                        load_idx(b + 2)
                        load_q(b + 2)
                    if b == 0:
                        for i in range(5, S_ITEM):
                            load_item(i)
                    if 1 <= b < 4:
                        load_item(S_ITEM + b - 1)
                    if b >= 1:
                        q0, Tq = rows(b - 1)
                        sp.wait_ge(s["res_ok"], 2 * b)
                        go(xs[l + 1, q0:q0 + Tq, :], xr[0:Tq, (b - 1) % 2, :], f"b_st{(b - 1) % 2}")
                    if 2 <= b + 1 < NBLK:
                        load_yx(b + 1)
                sp.wait_ge(s["res_ok"], 2 * NBLK)
                go(xs[l + 1, r0:r0 + T, :], xr[0:T, (NBLK - 1) % 2, :], f"b_st{(NBLK - 1) % 2}")
                sp.wait_ge(s["b_st0"], 16 * ((NBLK + 1) // 2))
                sp.wait_ge(s["b_st1"], 16 * (NBLK // 2))

            @block.tensor
            def _(pe):
                mm = nc.tensor.matmul
                uses = []

                def bank(reader):
                    n = len(uses)
                    if n >= 4:
                        pe.wait_ge(*uses[n - 4])
                    uses.append(reader)
                    return SC[n % 4]

                def wait_pairs(i):
                    if i < S_ITEM:
                        pe.wait_ge(s["hi_ok"], i + 1)
                    pe.wait_ge(*paired(i))

                def logit_maxima(b):
                    c, W, _ = keys_of(b)
                    T = rows(b)[1]
                    n = before(b, n_qk)
                    pe.wait_ge(s["q16_ok"], 2 * b + 2)
                    if b == 0:
                        wait_pairs(1)
                    if b == NB:
                        wait_pairs(items.index(("s", 1)))
                    for c0, wd in tiles(W):
                        for h in range(8):
                            n += 1
                            ps = bank((s["max_ok"], n))
                            mm(ps[0:T, 0:wd], q16[:, b % 2, h * T:(h + 1) * T], keys[c][h // GRP][0][:, c0:c0 + wd],
                               start=True, stop=True).then_inc(s["qk_ok"], 1)

                idx_seen = []

                def indexer(b):
                    c, W, _ = keys_of(b)
                    T = rows(b)[1]
                    if not searched(b):
                        return
                    n = before(b, n_idx)
                    pe.wait_ge(s["iq16_ok"], 2 * idx_nth(b))
                    if c not in idx_seen:
                        wait_pairs(items.index(("ps"[c], 2)))
                        idx_seen.append(c)
                    for h, c0, wd, _ in idx_order(W):
                        n += 1
                        ps = bank((s["relu_ok"], n))
                        mm(ps[0:T, 0:wd], iq16[:, b % 2, h * T:(h + 1) * T], keys[c][2][0][:, c0:c0 + wd],
                           start=True, stop=False)
                        mm(ps[0:T, 0:wd], iq16[:, b % 2, h * T:(h + 1) * T], keys[c][2][1][:, c0:c0 + wd],
                           start=False, stop=True).then_inc(s["idx_ok"], 1)

                def attention(b):
                    c, W, _ = keys_of(b)
                    T = rows(b)[1]
                    pe.wait_ge(s["md_ok"], b + 1)
                    pe.wait_ge(s["mneg_ok"], b + 1)
                    if b >= 1:
                        pe.wait_ge(s["oT_ok"], 2 * b)
                    if b == 0:
                        pe.wait_ge(s["b_vp"], 32)
                    if b == NB:
                        pe.wait_ge(s["b_vs"], 64)
                    base = before(b, n_main)
                    steps = [(k0, kw, kv) for k0, kw in key_blocks(W) for kv in range(2)]

                    def logits(i):
                        k0, kw, kv = steps[i]
                        ps = bank((s["exp_ok"], base + i + 1))
                        q = q16[:, b % 2, kv * 4 * T:(kv + 1) * 4 * T]
                        mm(ps[0:kw, 0:4 * T], keys[c][kv][0][:, k0:k0 + kw], q, start=True, stop=False)
                        mm(ps[0:kw, 0:4 * T], keys[c][kv][1][:, k0:k0 + kw], q, start=False, stop=False)
                        mm(ps[0:kw, 0:4 * T], mneg[b % 2][0:T, k0:k0 + kw], identb[0:T, :, 0:T], start=False, stop=False)
                        mm(ps[0:kw, 0:4 * T], onesb[0:T, 0:kw], md[0:T, 4 * kv:4 * kv + 4, 0:T],
                           start=False, stop=True).then_inc(s["qkt_ok"], 1)

                    def values(i):
                        k0, kw, kv = steps[i]
                        pe.wait_ge(s["exp_ok"], base + i + 1)
                        mm(PV[kv][0:HD + 1, 0:4 * T], va[c][0:kw, k0 // P, kv, :], pt[0:kw, (base + i) % 4, 0:4 * T],
                           start=(k0 == 0), stop=(k0 + kw == W)).then_inc(s["pv_ok"], 1)

                    AHEAD = 3
                    for i in range(min(AHEAD, len(steps))):
                        logits(i)
                    for i in range(len(steps)):
                        if i + AHEAD < len(steps):
                            logits(i + AHEAD)
                        values(i)

                def out_transposes(b):
                    T = rows(b)[1]
                    pe.wait_ge(s["oT_ok"], 2 * b + 2)
                    if b >= 1:
                        pe.wait_ge(s["res_ok"], 2 * b)
                    for kv in range(2):
                        for p in range(4):
                            last = nc.tensor.transpose(X[kv][0:T, p * P:p * P + HD + 1],
                                                       oT[0:HD + 1, kv, p * T:(p + 1) * T], ident[0:HD + 1, 0:HD + 1])
                        last.then_inc(s["oX_ok"], 1)

                def mixed_transposes(b):
                    T = rows(b)[1]
                    pe.wait_ge(s["on_ok"], b + 1)
                    for c in range(DC):
                        last = nc.tensor.transpose(X[c // 4][:, (c % 4) * P:(c % 4) * P + T],
                                                   yt[0:T, b % 2, c * P:(c + 1) * P], ident[0:T, 0:T])
                    last.then_inc(s["yX_ok"], 1)

                def project(b):
                    T = rows(b)[1]
                    pe.wait_ge(s["yTl_ok"], 2 * b + 2)
                    if b == 0:
                        wait_pairs(items.index(("w", DC // 2 - 1)))
                    for n in range(2):
                        cols = slice(n * 512, (n + 1) * 512)
                        for c in range(DC):
                            mm(X[n][0:T, :], yTh[:, c, 0:T], wo[0][:, c, cols], start=(c == 0), stop=False)
                            mm(X[n][0:T, :], yTh[:, c, 0:T], wo[1][:, c, cols], start=False, stop=False)
                            last = mm(X[n][0:T, :], yTl[:, c, 0:T], wo[0][:, c, cols], start=False, stop=(c == DC - 1))
                        last.then_inc(s["op_ok"], 1)

                pe.wait_ge(s["b_prep"], 1)
                indexer(0)
                for b in range(NBLK):
                    logit_maxima(b)
                    if b >= 1:
                        out_transposes(b - 1)
                    if b + 1 < NBLK:
                        indexer(b + 1)
                    if b >= 1:
                        mixed_transposes(b - 1)
                        project(b - 1)
                    attention(b)
                out_transposes(NBLK - 1)
                mixed_transposes(NBLK - 1)
                project(NBLK - 1)

            @block.scalar
            def _(act):
                A = nc.scalar.activation

                def indexer(b):
                    if not searched(b):
                        return
                    T = rows(b)[1]
                    n = before(b, n_idx)
                    for h, c0, wd, _ in idx_order(keys_of(b)[1]):
                        n += 1
                        act.wait_ge(s["idx_ok"], n)
                        if n > 4:
                            act.wait_ge(s["acc_ok"], n - 4)
                        A(rl[0:T, (n - 1) % 4, 0:wd], sc_bank()[0:T, 0:wd], ACT.Relu).then_inc(s["relu_ok"], 1)

                count = [0]

                def sc_bank():
                    count[0] += 1
                    return SC[(count[0] - 1) % 4]

                def skip_maxima(b):
                    count[0] += n_qk(b)

                def side_by_side(b):
                    T, base = rows(b)[1], before(b, n_main)
                    widths = [kw for _, kw in key_blocks(keys_of(b)[1]) for _ in range(2)]
                    for kind, i in order(b):
                        if kind == "bisect":
                            count_scores(b + 1, i)
                            continue
                        exponential(base + i + 1, widths[i], T)
                        if i + 1 == len(widths):
                            outputs(b, base + i + 1, T)

                def exponential(n, kw, T):
                    act.wait_ge(s["qkt_ok"], n)
                    if n > 4:
                        act.wait_ge(s["pv_ok"], n - 4)
                    A(pt[0:kw, (n - 1) % 4, 0:4 * T], sc_bank()[0:kw, 0:4 * T], ACT.Exp,
                      scale=HD ** -0.5).then_inc(s["exp_ok"], 1)

                def outputs(b, n, T):
                    if b >= 1:
                        act.wait_ge(s["oX_ok"], 2 * b)
                    for kv in range(2):
                        act.wait_ge(s["pv_ok"], n - 1 + kv)
                        A(oT[0:HD + 1, kv, 0:4 * T], PV[kv][0:HD + 1, 0:4 * T], ACT.Copy).then_inc(s["oT_ok"], 1)

                def count_scores(b, i):
                    W, T = keys_of(b)[1], rows(b)[1]
                    n = NIT * (idx_nth(b) - 1) + i + 1
                    act.wait_ge(s["mid_ok"], n)
                    if b >= 2 and i == 0:
                        act.wait_ge(s["mneg_ok"], b)
                    w0 = W - act_share(W)
                    A(ghi[0:T, w0:W], sc[b % 2][0:T, w0:W], ACT.Sign, scale=-1.0, bias=small["mid"][0:T, :],
                      accum_out=small["cnta"][0:T, :]).then_inc(s["cnt_ok"], 1)

                def mixed_copies(b):
                    T = rows(b)[1]
                    act.wait_ge(s["yX_ok"], b + 1)
                    if b >= 1:
                        act.wait_ge(s["op_ok"], 2 * b)
                    for n in range(2):
                        A(yTh[:, 4 * n:4 * n + 4, 0:T], X[n][:].rearrange("p (c t) -> p c t", c=4)[:, :, 0:T],
                          ACT.Copy).then_inc(s["yTh_ok"], 1)

                def high_halves(i0, i1):
                    for i in range(i0, i1):
                        act.wait_ge(*staged(i))
                        src, hi, _, scale = pair_of(i)
                        A(hi, src, ACT.Copy, scale=scale).then_inc(s["hi_ok"], 1)

                high_halves(0, W_ITEM)
                indexer(0)
                if searched(0):
                    for i in range(NIT):
                        count_scores(0, i)
                for b in range(NBLK):
                    skip_maxima(b)
                    if b + 1 < NBLK:
                        indexer(b + 1)
                    if b == 1:
                        high_halves(W_ITEM + 2, S_ITEM)
                    if b >= 1:
                        mixed_copies(b - 1)
                    side_by_side(b)
                    if b == 0:
                        high_halves(W_ITEM, W_ITEM + 2)
                mixed_copies(NBLK - 1)

            @block.gpsimd
            def _(pool):
                G = nc.gpsimd
                G.memset(va[0][:, :, :, HD:HD + 1], 2.0 * W_SCALE)
                G.memset(va[1][:, :, :, HD:HD + 1], 2.0 * W_SCALE)
                G.memset(onesb[:], 1.0)
                for i in range(4):
                    last = G.tensor_copy(identb[:, i, :], ident[:])
                last.then_inc(s["b_prep"], 1)

                def split_queries(dst, src, T, done, value):
                    G.tensor_copy(dst[:, 0:8 * T], src[:, 0:8 * T]).then_inc(done, 1)
                    pool.wait_ge(done, 2 * value - 1)
                    G.tensor_tensor(dst[HD:P, 0:8 * T], src[HD:P, 0:8 * T], dst[HD:P, 0:8 * T], ALU.subtract).then_inc(done, 1)
                    pool.wait_ge(done, 2 * value)

                def split_q(b):
                    pool.wait_ge(s["b_q"], 64 * (b + 1))
                    if b >= 2:
                        pool.wait_ge(s["qkt_ok"], before(b - 1, n_main))
                    split_queries(q16[:, b % 2], qs, rows(b)[1], s["q16_ok"], b + 1)

                def split_iq(b):
                    if not searched(b):
                        return
                    pool.wait_ge(s["b_iq"], 64 * idx_nth(b))
                    if b >= 2 and searched(b - 2):
                        pool.wait_ge(s["idx_ok"], before(b - 1, n_idx))
                    split_queries(iq16[:, b % 2], iqs, rows(b)[1], s["iq16_ok"], idx_nth(b))

                def make_pairs(i):
                    pool.wait_ge(*staged(i))
                    src, hi, lo, _ = pair_of(i)
                    G.tensor_copy(hi, src).then_inc(s["pair_hi"], 1)
                    pool.wait_ge(s["pair_hi"], i - S_ITEM + 1)
                    G.tensor_tensor(lo, src, hi, ALU.subtract).then_inc(s["pair_ok"], 1)

                def max_diagonals(b):
                    T = rows(b)[1]
                    pool.wait_ge(s["mx_ok"], b + 1)
                    if b >= 1:
                        pool.wait_ge(s["qkt_ok"], before(b, n_main))
                    G.tensor_tensor(md[0:T, :, 0:T], identb[0:T, 0, 0:T].unsqueeze(1).broadcast_to([T, 8, T]),
                                    mx[0:T, :].unsqueeze(2).broadcast_to([T, 8, T]), ALU.mult).then_inc(s["md_ok"], 1)

                split_q(0)
                split_iq(0)
                split_iq(1)
                split_q(1)
                for b in range(NBLK):
                    max_diagonals(b)
                    if b + 2 < NBLK:
                        split_iq(b + 2)
                    if 1 <= b < 4:
                        make_pairs(S_ITEM + b - 1)
                    if b + 2 < NBLK:
                        split_q(b + 2)

            @block.vector
            def _(dve):
                V = nc.vector
                step = Steps(dve, s["b_step"])
                count = [0]

                def sc_bank():
                    count[0] += 1
                    return SC[(count[0] - 1) % 4]

                def maxima(b):
                    c, W, _ = keys_of(b)
                    T = rows(b)[1]
                    n = before(b, n_qk)
                    nt = len(tiles(W))
                    for j, (c0, wd) in enumerate(tiles(W)):
                        for h in range(8):
                            n += 1
                            dve.wait_ge(s["qk_ok"], n)
                            if n > 2:
                                dve.wait_ge(s["max_ok"], n - 2)
                            V.tensor_tensor_reduce(out=junk[0:T, n % 2, 0:wd], in0=sc_bank()[0:T, 0:wd],
                                                   in1=mneg[b % 2][0:T, c0:c0 + wd], scale=1.0, scalar=-3e38,
                                                   op0=ALU.add, op1=ALU.max,
                                                   accum_out=mxt[0:T, h, j:j + 1]).then_inc(s["max_ok"], 1)
                    dve.wait_ge(s["max_ok"], n)
                    if b >= 1:
                        dve.wait_ge(s["md_ok"], b)
                    step(V.tensor_reduce(mx[0:T, :], mxt[0:T, :, 0:nt], AX_X, ALU.max))
                    V.tensor_scalar(mx[0:T, :], mx[0:T, :], -1.0, None, ALU.mult).then_inc(s["mx_ok"], 1)

                def normalise(b):
                    T = rows(b)[1]
                    dve.wait_ge(s[f"b_y{b % 2}"], 16 * (b // 2 + 1))
                    dve.wait_ge(s["oX_ok"], 2 * b + 2)
                    for kv in range(2):
                        x3 = X[kv][0:T, :].rearrange("p (h d) -> p h d", h=4)
                        step(V.reciprocal(rs[0:T, 4 * kv:4 * kv + 4], x3[:, :, HD]))
                        step(V.tensor_tensor(on[0:T, 256 * kv:256 * kv + 256].rearrange("p (h d) -> p h d", h=4),
                                             x3[:, :, 0:HD], rs[0:T, 4 * kv:4 * kv + 4].unsqueeze(2)
                                             .broadcast_to([T, 4, HD]), ALU.mult))
                    V.tensor_tensor(yt[0:T, b % 2, 0:512], yt[0:T, b % 2, 0:512], on[0:T, :], ALU.mult).then_inc(s["on_ok"], 1)

                def accumulate(b):
                    if not searched(b):
                        return
                    T = rows(b)[1]
                    n = before(b, n_idx)
                    count[0] += n_idx(b)
                    dst = sc[b % 2]
                    dve.wait_ge(s[f"b_iw{b % 2}"], 16 * idx_load(b))
                    for h, c0, wd, back in idx_order(keys_of(b)[1]):
                        n += 1
                        dve.wait_ge(s["relu_ok"], n)
                        src, w1 = rl[0:T, (n - 1) % 4, 0:wd], iw[0:T, b % 2, h:h + 1]
                        o = dst[0:T, c0:c0 + wd]
                        if h == 0:
                            V.tensor_scalar(o, src, w1, None, ALU.mult).then_inc(s["acc_ok"], 1)
                        else:
                            dve.wait_ge(s["acc_ok"], n - back)
                            V.scalar_tensor_tensor(out=o, in0=src, scalar=w1, in1=o, op0=ALU.mult,
                                                   op1=ALU.add).then_inc(s["acc_ok"], 1)
                    dve.wait_ge(s["acc_ok"], n)

                def low_halves(b):
                    T = rows(b)[1]
                    if b >= 1:
                        dve.wait_ge(s["op_ok"], 2 * b)
                    for n in range(2):
                        dve.wait_ge(s["yTh_ok"], 2 * b + n + 1)
                        V.tensor_tensor(yTl[:, 4 * n:4 * n + 4, 0:T], X[n][:].rearrange("p (c t) -> p c t", c=4)[:, :, 0:T],
                                        yTh[:, 4 * n:4 * n + 4, 0:T], ALU.subtract).then_inc(s["yTl_ok"], 1)

                def add_residual(b):
                    T = rows(b)[1]
                    dve.wait_ge(s[f"b_x{b % 2}"], 16 * (b // 2 + 1))
                    for n in range(2):
                        dve.wait_ge(s["op_ok"], 2 * b + n + 1)
                        o = xr[0:T, b % 2, n * 512:(n + 1) * 512]
                        V.scalar_tensor_tensor(out=o, in0=X[n][0:T, :], scalar=1.0 / W_SCALE, in1=o, op0=ALU.mult,
                                               op1=ALU.add).then_inc(s["res_ok"], 1)

                def select(b):
                    c, W, K = keys_of(b)
                    T = rows(b)[1]
                    out = mneg[b % 2][0:T, 0:W]
                    if b >= 2:
                        dve.wait_ge(s["qkt_ok"], before(b - 1, n_main))
                    if not searched(b):
                        step(V.memset(out, 0.0))
                        V.memset(mneg[b % 2][0:CHUNK, W - CHUNK:W], -MASKED).then_inc(s["mneg_ok"], 1)
                        dve.wait_ge(s["mneg_ok"], b + 1)
                        return
                    v = {n: t[0:T, :] for n, t in small.items()}
                    x = sc[b % 2][0:T, 0:W]
                    lo, hi, mid = v["lo"], v["hi"], v["mid"]
                    step(V.tensor_reduce(v["rng"], x, AX_X, ALU.max, apply_absolute_value=True))
                    step(V.tensor_scalar(v["rng"], v["rng"], 1e-30, 2.0, ALU.max, ALU.mult))
                    step(V.tensor_scalar(v["rng"].bitcast(I32), v["rng"].bitcast(I32), 0x7F800000, None, ALU.bitwise_and))
                    step(V.tensor_scalar(stp[0:T, :], pw[0:T, :], v["rng"], None, ALU.mult))
                    if b < NB:
                        step(V.memset(sc[b % 2][0:CHUNK, W - CHUNK:W], -BIG))
                    n = NIT * (idx_nth(b) - 1)
                    W_D = W - act_share(W)
                    V.memset(mid, 0.0).then_inc(s["mid_ok"], 1)
                    for i in range(NIT):
                        dve.wait_ge(s["mid_ok"], n + i + 1)
                        step(V.tensor_scalar(out[:, 0:W_D], x[:, 0:W_D], mid, None, ALU.is_ge, ALU.add, accum_out=v["cnt"]))
                        dve.wait_ge(s["cnt_ok"], n + i + 1)
                        step(V.scalar_tensor_tensor(out=v["cnt2"], in0=v["cnt"], scalar=2.0, in1=v["cnta"],
                                                    op0=ALU.mult, op1=ALU.subtract))
                        step(V.tensor_scalar(v["dlt"], v["cnt2"], float(2 * K - (W - W_D)), stp[0:T, i:i + 1],
                                             ALU.is_ge, ALU.mult))
                        ins = V.scalar_tensor_tensor(out=mid, in0=v["dlt"], scalar=stp[0:T, i + 1:i + 2], in1=mid,
                                                     op0=ALU.subtract, op1=ALU.add)
                        if i < NIT - 1:
                            ins.then_inc(s["mid_ok"], 1)
                        else:
                            step(ins)
                    step(V.tensor_tensor(lo, mid, stp[0:T, NIT:NIT + 1], ALU.subtract))
                    step(V.tensor_tensor(hi, mid, stp[0:T, NIT:NIT + 1], ALU.add))
                    step(V.tensor_scalar(out, x, lo, None, ALU.is_ge))
                    step(V.tensor_scalar(ghi[0:T, 0:W], x, hi, None, ALU.is_gt, ALU.add, accum_out=v["chi"]))
                    step(V.tensor_scalar(v["need"], v["chi"], -1.0, float(K), ALU.mult, ALU.add))
                    step(V.tensor_tensor_scan(x, out, ghi[0:T, 0:W], 0.0, ALU.add, ALU.subtract))
                    step(V.scalar_tensor_tensor(out=out, in0=x, scalar=v["need"], in1=out,
                                                op0=ALU.is_le, op1=ALU.mult))
                    step(V.tensor_tensor(out, out, ghi[0:T, 0:W], ALU.max))
                    V.tensor_scalar(out, out, -1.0, MASKED, ALU.add, ALU.mult).then_inc(s["mneg_ok"], 1)
                    dve.wait_ge(s["mneg_ok"], b + 1)

                def skip_main(b):
                    count[0] += n_main(b)

                def low_of_items(i0, i1):
                    for i in range(i0, i1):
                        dve.wait_ge(s["hi_ok"], i + 1)
                        src, hi, lo, scale = pair_of(i)
                        V.scalar_tensor_tensor(out=lo, in0=src, scalar=scale, in1=hi, op0=ALU.mult,
                                               op1=ALU.subtract).then_inc(s["lo_ok"], 1)

                low_of_items(0, W_ITEM)
                dve.wait_ge(s["b_const"], 16)
                accumulate(0)
                select(0)
                for b in range(NBLK):
                    maxima(b)
                    if b >= 1:
                        normalise(b - 1)
                    if b + 1 < NBLK:
                        accumulate(b + 1)
                    if b == 1:
                        low_of_items(W_ITEM + 2, S_ITEM)
                    if b >= 1:
                        low_halves(b - 1)
                    skip_main(b)
                    if b + 1 < NBLK:
                        select(b + 1)
                    if b == 0:
                        low_of_items(W_ITEM, W_ITEM + 2)
                    if b >= 1:
                        add_residual(b - 1)
                normalise(NBLK - 1)
                low_halves(NBLK - 1)
                add_residual(NBLK - 1)

    with ExitStack() as whole:
        def sem(name):
            return whole.enter_context(nc.semaphore(name))

        ident = whole.enter_context(nc.sbuf_tensor("ident", [P, P], F32))
        oml = whole.enter_context(nc.sbuf_tensor("oml", [P, DEPTH, 2], F32))
        lbt = whole.enter_context(nc.sbuf_tensor("lbt", [P, DEPTH, 2], F32))

        copied, lb_in, lb_step, lb_exp = sem("copied"), sem("lb_in"), sem("lb_step"), sem("lb_exp")
        with ExitStack() as ctx:
            lg = ctx.enter_context(nc.sbuf_tensor("lg", [P, DEPTH, 2], F32))
            mx = ctx.enter_context(nc.sbuf_tensor("lmx", [P, 2], F32))
            block = ctx.enter_context(nc.Block())

            @block.sync
            def _(sp):
                sp.dma_start(lg[:], lb_logits[:, :, :]).then_inc(lb_in, 16)
                sp.dma_start(ident[:], c_ident[:, :]).then_inc(lb_in, 16)
                sp.dma_start(xs[0, :, :], xin[:, :]).then_inc(copied, 16)
                sp.wait_ge(copied, 16)
                sp.wait_ge(lb_in, 32)

            @block.scalar
            def _(act):
                act.wait_ge(lb_exp, 1)
                nc.scalar.activation(lg[:], lg[:], ACT.Exp).then_inc(lb_exp, 1)

            @block.vector
            def _(dve):
                step = Steps(dve, lb_step)
                dve.wait_ge(lb_in, 32)
                step(nc.vector.tensor_copy(mx[:], lg[:, 0, :]))
                for l in range(1, DEPTH):
                    step(nc.vector.tensor_tensor(mx[:], mx[:], lg[:, l, :], ALU.max))
                for l in range(DEPTH):
                    step(nc.vector.tensor_tensor(lg[:, l, :], lg[:, l, :], mx[:], ALU.subtract))
                nc.vector.memset(lbt[:, 0, :], 0.0).then_inc(lb_exp, 1)
                dve.wait_ge(lb_exp, 2)
                step(nc.vector.tensor_copy(mx[:], lg[:, 0, :]))
                for l in range(1, DEPTH):
                    step(nc.vector.tensor_tensor(mx[:], mx[:], lg[:, l, :], ALU.add))
                step(nc.vector.reciprocal(mx[:], mx[:]))
                for l in range(DEPTH):
                    step(nc.vector.tensor_tensor(lg[:, l, :], lg[:, l, :], mx[:], ALU.mult))
                for l in range(1, DEPTH):
                    step(nc.vector.tensor_tensor(lbt[:, l, :], lbt[:, l - 1, :], lg[:, l, :], ALU.add))
                step(nc.vector.tensor_scalar(oml[:], lbt[:], -1.0, 1.0, ALU.mult, ALU.add))

        sems = {}

        def layer_sem(name):
            if name not in sems:
                sems[name] = sem(name)
            return sems[name]

        with nc.Fori(0, DEPTH) as l:
            recurrent_half(l, layer_sem)
            attention_half(l, layer_sem)
            with nc.Block() as block:
                @block.gpsimd
                def _(pool):
                    for s in sems.values():
                        pool.sem_clear(s)



def shape_constants(seq, past, ts):
    nb = seq // P
    half = HD // 2
    pos = np.zeros((nb + 1, P), np.float32)
    pos[:nb] = np.arange(seq, dtype=np.float32).reshape(nb, P)
    pos[nb, :ts] = past + np.arange(ts)
    freq = (10000.0 ** (-np.arange(half, dtype=np.float64) / half)).astype(np.float32)
    ang = (pos[:, :, None] * freq).astype(np.float32).astype(np.float64)
    rope = np.concatenate([np.cos(ang), np.sin(ang)], -1).astype(np.float32).transpose(1, 0, 2)
    lg = np.log(1.0 - np.exp(np.linspace(np.log(1.0 / 32), np.log(1.0 / 512), 4)))
    n = np.arange(P)
    diff = n[None, :] - n[:, None]
    dmat = np.where(diff[:, None, :] >= 0, np.exp(np.maximum(diff, 0)[:, None, :] * lg[None, :, None]), 0.0) * HD ** -0.5
    lrow = np.zeros((P, 2, P))
    ksc = np.zeros((P, 2, 4))
    gt = np.zeros((P, 2, 2))
    for p in range(2):
        for j in range(2):
            r = slice(64 * j, 64 * j + 64)
            lrow[r, p, :] = np.exp((n + 1.0) * lg[2 * p + j])
            for v, T in enumerate((P, ts)):
                gt[r, v, p] = np.exp(T * lg[2 * p + j])
    for v, T in enumerate((P, ts)):
        ksc[:T, v, :] = np.exp((T - 1.0 - n[:T])[:, None] * lg[None, :]) * HD ** -0.5
    bmask = np.kron(np.eye(2), np.ones((64, 64)))
    causal = (diff >= 0)
    return [np.ascontiguousarray(a.astype(np.float32)) for a in
            (rope, np.eye(P), causal, dmat, lrow, ksc, gt, bmask,
             np.broadcast_to(2.0 ** -np.arange(NIT + 1), (P, NIT + 1)))]


def column_order():
    sizes = [("aq", 512), ("ak", 128), ("av", 128), ("ag", 512), ("iq", 512), ("ik", 64), ("iw", 8), ("bq", 256),
             ("bf", 256), ("bi", 256), ("bg", 256), ("cq", 256), ("ck", 256), ("cv", 256), ("cg", 256)]
    at, cols = 0, {}
    for n, wd in sizes:
        cols[n] = np.arange(at, at + wd)
        at += wd
    pairs = [h for p in range(4) for h in (p, p + 4)]
    for n in ("aq", "iq"):
        cols[n] = cols[n].reshape(8, HD)[pairs].ravel()
    parts = {"bqf": "bq bf", "big": "bi bg", "cqk": "cq ck", "cvg": "cv cg", "iq": "iq", "kvi": "ak av ik iw",
             "aq": "aq", "ag": "ag"}
    return np.concatenate([cols[c] for n, _ in GROUPS for c in parts[n].split()])


def kernel(x_prompt, x_sample, cache_k, cache_v, cache_idx_k, state_hgrn, state_ret, norm_g, w_in, q_norm_g,
           k_norm_g, hgrn_lb_logits, hgrn_norm_g, ret_norm_g, w_out):
    import concourse.bacc as _bacc
    from concourse.bass_utils import run_bass_kernel_spmd as _run

    arr = [np.asarray(a) for a in (x_prompt, x_sample, cache_k, cache_v, cache_idx_k, state_hgrn, state_ret, norm_g,
                                   w_in, q_norm_g, k_norm_g, hgrn_lb_logits, hgrn_norm_g, ret_norm_g, w_out)]
    xp, xsm, ck, cv, ci, sh, sr, ng, wi, qg, kg, lb, hg, rg, wo = arr
    depth, d = ng.shape
    seq, ts, past = xp.shape[1], xsm.shape[1], ck.shape[2]

    def over_partitions(g):
        return np.broadcast_to(g[:, None, :], (depth, P, g.shape[1]))

    wi = wi[:, :, column_order()].reshape(depth, d // P, P, N_IN).transpose(0, 2, 1, 3)
    w_cols = np.concatenate([wi[..., GOFF[n]:GOFF[n] + wd].reshape(depth, P, -1) for n, wd in GROUPS], -1)
    ins = [np.concatenate([xp[0], xsm[0]], 0), ck.reshape(depth, past, 2 * HD).transpose(0, 2, 1),
           cv.reshape(depth, past // P, P, 2 * HD).transpose(0, 2, 1, 3), ci[:, 0].transpose(0, 2, 1), sh[:, 0], sr[:, 0],
           ng.reshape(depth, d // P, P).transpose(0, 2, 1),
           w_cols, over_partitions(qg), over_partitions(kg), lb.reshape(depth, 2, P).transpose(2, 0, 1), over_partitions(hg),
           over_partitions(rg),
           wo.reshape(depth, d // P, P, d).transpose(0, 2, 1, 3)] + shape_constants(seq, past, ts)
    outs = [(depth + 1, seq + ts, d), (depth, seq, 128), (depth, seq, 128), (depth, seq, HD), (depth, 4, HD, HD),
            (depth, 4, HD, HD), (depth, ts, 128), (depth, ts, 128), (depth, ts, HD), (depth, 4, HD, HD),
            (depth, 4, HD, HD)]
    nc = _bacc.Bacc("TRN2", target_bir_lowering=False, num_devices=1)
    arrays, args = {}, []
    for i, a in enumerate(ins):
        a = np.ascontiguousarray(a)
        arrays[f"in_{i}"] = a
        args.append(nc.dram_tensor(f"in_{i}", a.shape, mybir.dt.from_np(a.dtype), kind="ExternalInput").ap())
    for i, shape in enumerate(outs):
        args.append(nc.dram_tensor(f"out_{i}", shape, F32, kind="ExternalOutput").ap())
    build(nc, *args)
    r = _run(nc, [arrays], core_ids=[0]).results[0]
    x, k, v, ik, h, rt, ks, vs, iks, hs, rs = (r[f"out_{i}"] for i in range(len(outs)))
    y = x[depth]
    return (y[None, :seq], y[None, seq:], k.reshape(depth, 1, seq, 2, HD), v.reshape(depth, 1, seq, 2, HD),
            ik.reshape(depth, 1, seq, HD), h[:, None], rt[:, None], ks.reshape(depth, 1, ts, 2, HD),
            vs.reshape(depth, 1, ts, 2, HD), iks.reshape(depth, 1, ts, HD), hs[:, None], rs[:, None])
```
